# Optimizing a Trainium2 kernel written in Bass

```python
import math
import jax, jax.numpy as jnp
from jax import lax
import numpy as np

D_MODEL = 2048
BATCH = 1
SEQ = 256
DEPTH = 2

DIFF_HEADS = 8
DIFF_QK_DIM = 64
DIFF_V_DIM = 128
DIFF_WIDTH = DIFF_HEADS * DIFF_V_DIM
MLA_HEADS = 8
MLA_Q_RANK = 512
MLA_KV_RANK = 512
MLA_NOPE_DIM = 128
MLA_ROPE_DIM = 64
MLA_V_DIM = 128
MLA_WIDTH = MLA_HEADS * MLA_V_DIM
MIX_WIDTH = DIFF_WIDTH + MLA_WIDTH
IN_SIZES = (
    DIFF_HEADS * 2 * DIFF_QK_DIM,
    DIFF_HEADS * 2 * DIFF_QK_DIM,
    DIFF_WIDTH,
    DIFF_WIDTH,
    MLA_Q_RANK,
    MLA_KV_RANK,
    MLA_ROPE_DIM,
    MLA_WIDTH,
)
IN_WIDTH = sum(IN_SIZES)
ROPE_THETA = 10000.0
NUM_BUCKETS = 32
MAX_DISTANCE = 128
BLOCK_Q = 128
EPS = 1e-6
NEG_INF = -1e30


def _rms_norm(x, g):
    xf = x.astype(jnp.float32)
    y = xf * lax.rsqrt(jnp.mean(xf * xf, axis=-1, keepdims=True) + EPS)
    return (y * g.astype(jnp.float32)).astype(x.dtype)

def _rope_tables(seq):
    pos = jnp.arange(seq, dtype=jnp.float32)
    inv = 1.0 / (ROPE_THETA ** (jnp.arange(0, MLA_ROPE_DIM, 2, dtype=jnp.float32) / MLA_ROPE_DIM))
    ang = pos[:, None] * inv[None, :]
    ang = jnp.concatenate([ang, ang], axis=-1)
    return jnp.cos(ang), jnp.sin(ang)

def _apply_rope(x, cos, sin):
    half = x.shape[-1] // 2
    x1, x2 = x[..., :half], x[..., half:]
    rot = jnp.concatenate([-x2, x1], axis=-1)
    return x * cos.astype(x.dtype) + rot * sin.astype(x.dtype)

def _t5_bucket(dist):
    n = jnp.maximum(dist, 0)
    max_exact = NUM_BUCKETS // 2
    nf = jnp.maximum(n, 1).astype(jnp.float32)
    large = max_exact + (jnp.log(nf / max_exact) / math.log(MAX_DISTANCE / max_exact)
                         * (NUM_BUCKETS - max_exact)).astype(jnp.int32)
    large = jnp.minimum(large, NUM_BUCKETS - 1)
    return jnp.where(n < max_exact, n, large)

def _block_sweep(one_block, seq):
    starts = jnp.arange(seq // BLOCK_Q, dtype=jnp.int32) * BLOCK_Q
    out = lax.map(one_block, starts)
    out = jnp.moveaxis(out, 0, 1)
    b, nb, q, h, dv = out.shape
    return out.reshape(b, nb * q, h, dv)

def _diff_attention(q, k, v, lam, bias_table):
    seq = q.shape[1]
    kpos = jnp.arange(seq, dtype=jnp.int32)
    scale = DIFF_QK_DIM ** -0.5
    table = bias_table.astype(jnp.float32)

    def one_block(start):
        qb = lax.dynamic_slice_in_dim(q, start, BLOCK_Q, axis=1)
        s = jnp.einsum('bqhmd,bkhmd->bmhqk', qb, k).astype(jnp.float32) * scale
        dist = (start + jnp.arange(BLOCK_Q, dtype=jnp.int32))[:, None] - kpos[None, :]
        bias = jnp.transpose(table[_t5_bucket(dist)], (2, 0, 1))
        s = jnp.where((dist >= 0)[None, None, None], s + bias[None, None], NEG_INF)
        p = jax.nn.softmax(s, axis=-1)
        w = p[:, 0] - lam * p[:, 1]
        return jnp.einsum('bhqk,bkhd->bqhd', w.astype(v.dtype), v)

    return _block_sweep(one_block, seq)

def _mla_attention(q_nope, q_rope, k_nope, k_rope, v):
    seq = q_nope.shape[1]
    kpos = jnp.arange(seq, dtype=jnp.int32)
    scale = (MLA_NOPE_DIM + MLA_ROPE_DIM) ** -0.5

    def one_block(start):
        qn = lax.dynamic_slice_in_dim(q_nope, start, BLOCK_Q, axis=1)
        qr = lax.dynamic_slice_in_dim(q_rope, start, BLOCK_Q, axis=1)
        s = (jnp.einsum('bqhd,bkhd->bhqk', qn, k_nope)
             + jnp.einsum('bqhr,bkr->bhqk', qr, k_rope)).astype(jnp.float32) * scale
        dist = (start + jnp.arange(BLOCK_Q, dtype=jnp.int32))[:, None] - kpos[None, :]
        s = jnp.where((dist >= 0)[None, None], s, NEG_INF)
        p = jax.nn.softmax(s, axis=-1)
        return jnp.einsum('bhqk,bkhd->bqhd', p.astype(v.dtype), v)

    return _block_sweep(one_block, seq)

def first_inputs(seed: int = 0) -> dict:
    key = jax.random.key(seed)
    ks = jax.random.split(key, 12)
    f32 = jnp.float32
    x = jax.random.normal(ks[0], (BATCH, SEQ, D_MODEL), f32)
    norm_g = 1.0 + 0.02 * jax.random.normal(ks[1], (DEPTH, D_MODEL), f32)
    w_in = jax.random.normal(ks[2], (DEPTH, D_MODEL, IN_WIDTH), f32) * D_MODEL ** -0.5
    diff_lambda = 0.1 * jax.random.normal(ks[3], (DEPTH, 4, DIFF_QK_DIM), f32)
    diff_subln_g = 1.0 + 0.02 * jax.random.normal(ks[4], (DEPTH, DIFF_V_DIM), f32)
    rel_bias_table = 0.2 * jax.random.normal(ks[5], (NUM_BUCKETS, DIFF_HEADS), f32)
    mla_q_norm_g = 1.0 + 0.02 * jax.random.normal(ks[6], (DEPTH, MLA_Q_RANK), f32)
    w_uq = jax.random.normal(ks[7], (DEPTH, MLA_Q_RANK, MLA_HEADS * (MLA_NOPE_DIM + MLA_ROPE_DIM)), f32) * MLA_Q_RANK ** -0.5
    mla_kv_norm_g = 1.0 + 0.02 * jax.random.normal(ks[8], (DEPTH, MLA_KV_RANK), f32)
    w_ukv = jax.random.normal(ks[9], (DEPTH, MLA_KV_RANK, MLA_HEADS * (MLA_NOPE_DIM + MLA_V_DIM)), f32) * MLA_KV_RANK ** -0.5
    w_out = jax.random.normal(ks[10], (DEPTH, MIX_WIDTH, D_MODEL), f32) * MIX_WIDTH ** -0.5
    final_norm_g = 1.0 + 0.02 * jax.random.normal(ks[11], (D_MODEL,), f32)
    return {"x": x, "norm_g": norm_g, "w_in": w_in, "diff_lambda": diff_lambda,
            "diff_subln_g": diff_subln_g, "rel_bias_table": rel_bias_table,
            "mla_q_norm_g": mla_q_norm_g, "w_uq": w_uq, "mla_kv_norm_g": mla_kv_norm_g,
            "w_ukv": w_ukv, "w_out": w_out, "final_norm_g": final_norm_g}

def first_block(x, norm_g, w_in, diff_lambda, diff_subln_g, rel_bias_table,
              mla_q_norm_g, w_uq, mla_kv_norm_g, w_ukv, w_out, final_norm_g):
    b, seq, _ = x.shape
    cos, sin = _rope_tables(seq)
    split_points = [int(v) for v in np.cumsum(IN_SIZES)[:-1]]
    for l in range(DEPTH):
        h = _rms_norm(x, norm_g[l])
        proj = jnp.einsum('bsd,de->bse', h, w_in[l])
        q_a, k_a, v_a, z_a, c_q, c_kv, k_r, z_b = jnp.split(proj, split_points, axis=-1)

        lambda_init = 0.8 - 0.6 * math.exp(-0.3 * l)
        lp = diff_lambda[l].astype(jnp.float32)
        lam = (jnp.exp(jnp.sum(lp[0] * lp[1])) - jnp.exp(jnp.sum(lp[2] * lp[3])) + lambda_init)
        qa = q_a.reshape(b, seq, DIFF_HEADS, 2, DIFF_QK_DIM)
        ka = k_a.reshape(b, seq, DIFF_HEADS, 2, DIFF_QK_DIM)
        va = v_a.reshape(b, seq, DIFF_HEADS, DIFF_V_DIM)
        o_a = _diff_attention(qa, ka, va, lam, rel_bias_table)
        o_a = _rms_norm(o_a, diff_subln_g[l]) * (1.0 - lambda_init)
        o_a = o_a.reshape(b, seq, DIFF_WIDTH) * jax.nn.silu(z_a)

        q_b = jnp.einsum('bsr,re->bse', _rms_norm(c_q, mla_q_norm_g[l]), w_uq[l])
        q_b = q_b.reshape(b, seq, MLA_HEADS, MLA_NOPE_DIM + MLA_ROPE_DIM)
        q_nope, q_rope = q_b[..., :MLA_NOPE_DIM], q_b[..., MLA_NOPE_DIM:]
        q_rope = _apply_rope(q_rope, cos[:, None, :], sin[:, None, :])
        kv = jnp.einsum('bsr,re->bse', _rms_norm(c_kv, mla_kv_norm_g[l]), w_ukv[l])
        kv = kv.reshape(b, seq, MLA_HEADS, MLA_NOPE_DIM + MLA_V_DIM)
        k_nope, v_b = kv[..., :MLA_NOPE_DIM], kv[..., MLA_NOPE_DIM:]
        k_rope = _apply_rope(k_r, cos, sin)
        o_b = _mla_attention(q_nope, q_rope, k_nope, k_rope, v_b)
        o_b = o_b.reshape(b, seq, MLA_WIDTH) * jax.nn.silu(z_b)

        mixed = jnp.concatenate([o_a, o_b], axis=-1)
        x = x + jnp.einsum('bse,ed->bsd', mixed, w_out[l])
    return _rms_norm(x, final_norm_g)


DEPTH_2 = 1

N_MEM = 256
D_MIX = D_MODEL
D_CONV = 3 * D_MIX // 8
D_POOL = 3 * D_MIX // 8
D_XATT = D_MIX // 4
CONV_HEAD_DIM = 128
CONV_HEADS = D_CONV // CONV_HEAD_DIM
CONV_WIDTH = 3
POOL_WINDOWS = (2, 4, 8, 16)
POOL_GROUPS = len(POOL_WINDOWS)
POOL_GROUP_DIM = D_POOL // POOL_GROUPS
XATT_HEADS = 4
XATT_HEAD_DIM = D_XATT // XATT_HEADS
D_FF = ((8 * D_MODEL // 3 + 255) // 256) * 256
FFN_CONV_WIDTH = 3
D_IN = 3 * D_CONV + D_POOL + D_XATT


def rmsnorm(x, g):
    xf = x.astype(jnp.float32)
    y = xf * lax.rsqrt(jnp.mean(xf * xf, axis=-1, keepdims=True) + EPS)
    return (y * g.astype(jnp.float32)).astype(x.dtype)

def causal_dwconv(u, w):
    k = w.shape[0]
    s = u.shape[1]
    up = jnp.pad(u, ((0, 0), (k - 1, 0), (0, 0)))
    out = w[k - 1] * u
    for j in range(k - 1):
        out = out + w[j] * up[:, j:j + s]
    return out

def causal_pool_minus_self(v):
    s = v.shape[1]
    vf = v.astype(jnp.float32)
    c = jnp.pad(jnp.cumsum(vf, axis=1), ((0, 0), (1, 0), (0, 0), (0, 0)))
    t = jnp.arange(s, dtype=jnp.float32)[None, :, None]
    outs = []
    for g, k in enumerate(POOL_WINDOWS):
        cg = c[:, :, g]
        hi = cg[:, 1:]
        lo = jnp.pad(cg[:, :s + 1 - k], ((0, 0), (k - 1, 0), (0, 0)))
        cnt = jnp.minimum(t + 1.0, float(k))
        outs.append((hi - lo) / cnt - vf[:, :, g])
    return jnp.stack(outs, axis=2).astype(v.dtype)

def second_inputs(seed: int = 0) -> dict:
    key = jax.random.key(seed)
    ks = jax.random.split(key, 18)
    f32 = jnp.float32
    nrm = lambda k, shape, scale: (jax.random.normal(k, shape, f32) * scale)
    gain = lambda k, shape: 1.0 + 0.05 * jax.random.normal(k, shape, f32)
    L = DEPTH_2
    return {
        "x": jax.random.normal(ks[0], (BATCH, SEQ, D_MODEL), f32),
        "mem": jax.random.normal(ks[1], (BATCH, N_MEM, D_MODEL), f32),
        "g_mix": gain(ks[2], (L, D_MODEL)),
        "g_mem": gain(ks[3], (L, D_MODEL)),
        "w_in": nrm(ks[4], (L, D_MODEL, D_IN), D_MODEL ** -0.5),
        "conv_w": nrm(ks[5], (L, CONV_WIDTH, D_CONV), CONV_WIDTH ** -0.5),
        "pool_w": nrm(ks[6], (L, POOL_GROUPS, POOL_GROUP_DIM, POOL_GROUP_DIM), POOL_GROUP_DIM ** -0.5),
        "pool_scale": gain(ks[7], (L, D_POOL)),
        "w_kv": nrm(ks[8], (L, D_MODEL, 2 * D_XATT), D_MODEL ** -0.5),
        "w_out": nrm(ks[9], (L, D_MIX, D_MODEL), D_MIX ** -0.5),
        "g_ffn": gain(ks[10], (L, D_MODEL)),
        "w_up": nrm(ks[11], (L, D_MODEL, 2 * D_FF), D_MODEL ** -0.5),
        "ffn_conv_w": nrm(ks[12], (L, FFN_CONV_WIDTH, 2 * D_FF), FFN_CONV_WIDTH ** -0.5),
        "ffn_conv_b": nrm(ks[13], (L, 2 * D_FF), 0.01),
        "w_down": nrm(ks[14], (L, D_FF, D_MODEL), D_FF ** -0.5),
        "g_final": gain(ks[15], (D_MODEL,)),
    }

def second_block(x, mem, g_mix, g_mem, w_in, conv_w, pool_w, pool_scale, w_kv, w_out,
              g_ffn, w_up, ffn_conv_w, ffn_conv_b, w_down, g_final):
    b, s, _ = x.shape
    split_pts = [D_CONV, 2 * D_CONV, 3 * D_CONV, 3 * D_CONV + D_POOL]
    att_scale = 1.0 / math.sqrt(XATT_HEAD_DIM)
    for l in range(DEPTH_2):
        h = rmsnorm(x, g_mix[l])
        z = h @ w_in[l]
        cb, cc, cx, pv, q = jnp.split(z, split_pts, axis=-1)

        conv_out = cb * causal_dwconv(cc * cx, conv_w[l])

        pooled = causal_pool_minus_self(pv.reshape(b, s, POOL_GROUPS, POOL_GROUP_DIM))
        pool_out = jnp.einsum('bsgc,gcd->bsgd', pooled, pool_w[l]).reshape(b, s, D_POOL)
        pool_out = pool_out * pool_scale[l]

        m = rmsnorm(mem, g_mem[l])
        kv = m @ w_kv[l]
        k, v = jnp.split(kv, 2, axis=-1)
        k = k.reshape(b, N_MEM, XATT_HEADS, XATT_HEAD_DIM)
        v = v.reshape(b, N_MEM, XATT_HEADS, XATT_HEAD_DIM)
        qh = q.reshape(b, s, XATT_HEADS, XATT_HEAD_DIM)
        scores = jnp.einsum('bshd,bmhd->bhsm', qh, k).astype(jnp.float32) * att_scale
        probs = jax.nn.softmax(scores, axis=-1).astype(x.dtype)
        att = jnp.einsum('bhsm,bmhd->bshd', probs, v).reshape(b, s, D_XATT)

        mix = jnp.concatenate([conv_out, pool_out, att], axis=-1)
        x = x + mix @ w_out[l]

        h = rmsnorm(x, g_ffn[l])
        u = causal_dwconv(h @ w_up[l], ffn_conv_w[l]) + ffn_conv_b[l]
        gate, val = jnp.split(u, 2, axis=-1)
        x = x + (jax.nn.silu(gate) * val) @ w_down[l]
    return rmsnorm(x, g_final)


def setup_inputs(seed=0):
    out = dict(first_inputs(seed))
    for name, value in second_inputs(seed + 1).items():
        if name != "x":
            out[name + "_2"] = value
    return out


def reference(
    x, norm_g, w_in, diff_lambda, diff_subln_g, rel_bias_table, mla_q_norm_g, w_uq,
    mla_kv_norm_g, w_ukv, w_out, final_norm_g, mem_2, g_mix_2, g_mem_2, w_in_2, conv_w_2,
    pool_w_2, pool_scale_2, w_kv_2, w_out_2, g_ffn_2, w_up_2, ffn_conv_w_2, ffn_conv_b_2,
    w_down_2, g_final_2,
):
    x = first_block(
        x, norm_g, w_in, diff_lambda, diff_subln_g, rel_bias_table, mla_q_norm_g, w_uq,
        mla_kv_norm_g, w_ukv, w_out, final_norm_g,
    )
    return second_block(
        x, mem_2, g_mix_2, g_mem_2, w_in_2, conv_w_2, pool_w_2, pool_scale_2, w_kv_2, w_out_2,
        g_ffn_2, w_up_2, ffn_conv_w_2, ffn_conv_b_2, w_down_2, g_final_2,
    )


_drawn_inputs = setup_inputs


def setup_inputs(seed=0):
    import zlib

    import numpy as np

    out = dict(_drawn_inputs(seed))
    spreads = {}
    factors = {'diff_subln_g': 5.209,
     'mla_q_norm_g': 8.0,
     'mla_kv_norm_g': 8.0,
     'g_mem_2': 8.0,
     'ffn_conv_b_2': 22.634,
     'pool_scale_2': 7.294,
     'g_ffn_2': 4.304}
    for name, (base, spread) in spreads.items():
        noise = np.random.default_rng([zlib.crc32(name.encode()), seed]).standard_normal(out[name].shape)
        drawn = base * np.exp(spread * noise) if base else spread * noise
        out[name] = __import__('jax').numpy.asarray(drawn.astype(out[name].dtype))
    for name, factor in factors.items():
        out[name] = (out[name] * factor).astype(out[name].dtype)
    return out
```

```python
import math
from contextlib import ExitStack

import numpy as np

import concourse.bass as bass
from concourse import mybir
from concourse.alu_op_type import AluOpType as ALU

F32 = mybir.dt.float32
F32R = mybir.dt.float32r
BF16 = mybir.dt.bfloat16
I32 = mybir.dt.int32
ACT = mybir.ActivationFunctionType
AX_X = mybir.AxisListType.X

P = 128
SEQ = 256
T = SEQ // P
D = 2048
KT = D // P
LAYERS = 2
EPS = 1e-6
NEG = -1e30

HEADS = 8
DQ = 64
DV = 128
NOPE, ROPE = 128, 64
RANK = 512
WIDTH = HEADS * DV
COL_Q, COL_K, COL_V, COL_ZA = 0, WIDTH, 2 * WIDTH, 3 * WIDTH
COL_CQ = 4 * WIDTH
COL_CKV = COL_CQ + RANK
COL_KR = COL_CKV + RANK
COL_ZB = COL_KR + ROPE
IN_WIDTH = COL_ZB + WIDTH
UQ_WIDTH = HEADS * (NOPE + ROPE)
UKV_WIDTH = HEADS * (NOPE + DV)
DIFF_SCALE = DQ ** -0.5
MLA_SCALE = (NOPE + ROPE) ** -0.5
BUCKETS, MAX_DIST = 32, 128
THETA = 10000.0

D_CONV = 3 * D // 8
D_POOL = D_CONV
D_XATT = D // 4
XHEADS = 4
X_SCALE = (D_XATT // XHEADS) ** -0.5
WINDOWS = (2, 4, 8, 16)
GROUP = D_POOL // len(WINDOWS)
CT = D_CONV // P
D_FF = ((8 * D // 3 + 255) // 256) * 256
FT = D_FF // P
TAPS = 3

UNIT = 1024
RING = 4
LEAD = 3
U_MEM = 16
U_LAYER = 48 + 32 + 32 + 32
U_MIX = 14 * 4
U_OUT = 32
U_FFN = 8
N_FFN = D_FF // 256
U_DOWN = 4 * (FT // 2)
U_ALL = U_MEM + LAYERS * U_LAYER + U_MIX + U_OUT + N_FFN * U_FFN + U_DOWN
C_MEM, C_LAYER = 2, 24

G_NORM = 0
G_MIX = G_NORM + LAYERS * KT
G_FFN = G_MIX + KT
G_Q = G_FFN + KT
G_KV = G_Q + LAYERS * 4
G_POOL = G_KV + LAYERS * 4
G_CONV = G_POOL + CT
G_MEM = G_CONV + TAPS * CT
G_SUBLN = G_MEM + KT
G_ROWS = G_SUBLN + LAYERS
G_FIN = G_ROWS
G_ALL = G_FIN + KT
FFN_ROWS = 2 * FT
assert G_ROWS <= P and FFN_ROWS <= P

TURNS_PRO = 2 * 8 - 2
TB_PRO = TURNS_PRO + 1
TB_LAYER = 39
GAIN_LAYER = 12
TURN_LAYER = 20
DIFF_TB = [2, 3, 4, 7, 8, 11, 12, 13]
C_TURN = {10: (0, 0, 5), 11: (0, 1, 6), 18: (1, 0, 9), 19: (1, 1, 10)}
QR_TB, KR_TB = 14, 16
MLA_TB = [17, 18, 19, 22, 23, 26, 27, 30]
GATE_TURN = {12: (0, 0, 20), 13: (0, 1, 21), 20: (1, 0, 24), 21: (1, 1, 25), 28: (2, 0, 28), 29: (2, 1, 29),
             36: (3, 0, 31), 37: (3, 1, 32)}
X_TB = 33
DVE_STEPS_LAYER = 89
FIRST_FFN_STEPS, FFN_STEPS = 13, 17
X_SCORE, X_TURN, X_OUT = [52, 53, 56, 57], [55, 57, 59, 61], [56, 58, 60, 62]
POOL_OUT = [53, 54, 55]
MIX_TILES = [6, 8, 10, 12, 14, 16, 0, 2, 4, 18, 20, 22, 24, 26]
POOL_PIECES = [[(0, 0, 128), (1, 0, 64)], [(1, 64, 64), (2, 0, 128)],
               [(3, 0, 128), (4, 0, 64)], [(4, 64, 64), (5, 0, 128)]]
N_PIECES = sum(len(pieces) for pieces in POOL_PIECES)


def lam_init(layer):
    return 0.8 - 0.6 * math.exp(-0.3 * layer)


def shape_constants():
    ident = np.eye(P, dtype=np.float32)
    j = np.arange(SEQ + P)
    dist = SEQ - 1 - j
    n = np.maximum(dist, 0)
    half = BUCKETS // 2
    large = half + (np.log(np.maximum(n, 1) / half) / math.log(MAX_DIST / half) * half + 1e-9).astype(np.int64)
    bucket = np.where(n < half, n, np.minimum(large, BUCKETS - 1))
    onehot = ((bucket[None, :] == np.arange(BUCKETS)[:, None]) & (dist >= 0)[None, :]).astype(np.float32)
    future = np.broadcast_to(np.where(dist < 0, NEG, 0.0), (HEADS, SEQ + P)).astype(np.float32)
    q, k = np.arange(P)[:, None], np.arange(P)[None, :]
    causal = np.where(q - k >= 0, 0.0, NEG).astype(np.float32)
    inv = (1.0 / (THETA ** (np.arange(0, ROPE, 2, dtype=np.float32) / ROPE))).astype(np.float32)
    ang = np.arange(SEQ, dtype=np.float32)[:, None] * inv[None, :]
    rope = np.concatenate([np.cos(ang), np.cos(ang), -np.sin(ang), np.sin(ang)], axis=1)
    window = np.repeat(np.array(WINDOWS), GROUP).reshape(CT, P).T
    count = np.minimum(np.arange(16)[None, None, :] + 1, window[:, :, None])
    pool = np.concatenate([1.0 / window, (window[:, :, None] / count).reshape(P, -1)], axis=1)
    return {
        "c_ident": ident, "c_flip": np.ascontiguousarray(ident[::-1]), "c_onehot": onehot,
        "c_future": np.ascontiguousarray(future), "c_causal": causal,
        "c_rope": np.ascontiguousarray(rope.astype(np.float32)),
        "c_pool": np.ascontiguousarray(pool.astype(np.float32)),
    }


def build(nc, dram, out):
    k_tiled = lambda w: w.rearrange("l (k p) n -> p (l k) n", p=P)
    w_in, w_uq, w_ukv, w_out = (k_tiled(dram[n]) for n in ("w_in", "w_uq", "w_ukv", "w_out"))
    w_kv2, w_in2, w_out2, w_up2, w_down2 = (
        k_tiled(dram[n]) for n in ("w_kv_2", "w_in_2", "w_out_2", "w_up_2", "w_down_2"))
    by_token = lambda a: a.rearrange("b (t p) d -> p (b t) d", p=P)
    bias_dram = nc.dram_tensor("bias_by_distance", [HEADS, SEQ + P], F32, kind="Internal").ap()
    kv_dram = nc.dram_tensor("mem_kv", [P, T, 2 * D_XATT], F32, kind="Internal").ap()
    bias_rows = bass.AP(tensor=bias_dram.tensor, offset=0, ap=[[1, P], [SEQ + P, HEADS], [1, SEQ]])

    ctx = ExitStack()
    with ctx:
        def sb(name, shape, dt=F32, stack=ctx):
            return stack.enter_context(nc.sbuf_tensor("sb_" + name, shape, dt))

        def sem(name):
            return ctx.enter_context(nc.semaphore(name))

        stage = sb("stage", [P, RING, UNIT])
        w_hi = sb("w_hi", [P, RING, UNIT], F32R)
        w_lo = sb("w_lo", [P, RING, UNIT], F32R)
        x = sb("x", [P, T, D])
        xT = sb("xT", [P, KT, 2, SEQ], F32R)
        ident = sb("ident", [P, P])
        par = sb("par", [P, G_ALL])
        par_ffn = sb("par_ffn", [P, TAPS + 1, FFN_ROWS])
        turn_f32 = sb("turn_f32", [P, 2, 512])
        qkT = turn_f32[:, 1, :]
        sumsq_x = sb("sumsq_x", [P, T, 4])
        sumsq2 = sb("sumsq2", [P, T])
        rstd = sb("rstd", [P, T])
        newton_v = sb("newton_v", [P, 16])
        newton_t = sb("newton_t", [P, 16])
        junk = sb("junk", [P, 512], BF16)

        acc = ctx.enter_context(nc.psum_tensor("acc", [P, 4, 512], F32))
        aux = ctx.enter_context(nc.psum_tensor("aux", [P, 4, 512], F32))
        tb = aux[:, 0, :]
        sc1, sc0 = aux[:, 1, :], aux[:, 2, :]
        pv = aux[:, 3, :]

        staged = [sem(f"staged{i}") for i in range(RING)]
        hi_ready = sem("hi_ready")
        lo_ready = sem("lo_ready")
        unit_used = sem("unit_used")
        acc_free = [sem("acc_free0"), sem("acc_free1")]
        tb_filled, tb_free = sem("tb_filled"), sem("tb_free")
        turn_hi, turn_lo = sem("turn_hi"), sem("turn_lo")
        x_loaded, mem_loaded, par_loaded = sem("x_loaded"), sem("mem_loaded"), sem("par_loaded")
        ident_loaded, bias_loaded, consts_loaded = sem("ident_loaded"), sem("bias_loaded"), sem("consts_loaded")
        bias_out, bias_back, kv_out = sem("bias_out"), sem("bias_back"), sem("kv_out")
        mix_loaded, gfin_loaded, stored = sem("mix_loaded"), sem("gfin_loaded"), sem("stored")
        gmid_loaded = sem("gmid_loaded")
        par_filled, par_read = sem("par_filled"), sem("par_read")
        bias_filled, bias_read = sem("bias_filled"), sem("bias_read")
        dots_ready, exp_dots = sem("dots_ready"), sem("exp_dots")
        m_squared, rstd_m_ready = sem("m_squared"), sem("rstd_m_ready")
        x_squared, c_squared, o_squared = sem("x_squared"), sem("c_squared"), sem("o_squared")
        c_rstd = sem("c_rstd")
        x_normed = sem("x_normed")
        roped, pool_step = sem("roped"), sem("pool_step")
        scores_ready, row_max, exps_done = sem("scores_ready"), sem("row_max"), sem("exps_done")
        probs_ready, rsum_ready = sem("probs_ready"), sem("rsum_ready")
        pv_filled, pv_free = sem("pv_filled"), sem("pv_free")
        z_silu, gated = sem("z_silu"), sem("gated")
        rb_ready, rb_filled = sem("rb_ready"), sem("rb_filled")
        half_copied = sem("half_copied")
        conv_ready, conv_hi, conv_lo = sem("conv_ready"), sem("conv_hi"), sem("conv_lo")
        pool_zeroed = sem("pool_zeroed")
        pooled_ready, pool_filled, pool_scaled = sem("pooled_ready"), sem("pool_filled"), sem("pool_scaled")
        pool_hi, pool_lo = sem("pool_hi"), sem("pool_lo")
        queries_ready = sem("queries_ready")
        xs_ready, xmax_ready, xexp_done, xprob_ready = (
            sem("xs_ready"), sem("xmax_ready"), sem("xexp_done"), sem("xprob_ready"))
        xpt_filled, xpt_ready, xo_filled = sem("xpt_filled"), sem("xpt_ready"), sem("xo_filled")
        xo_hi, xo_lo = sem("xo_hi"), sem("xo_lo")
        gate_conv, gate_silu, act_ready = sem("gate_conv"), sem("gate_silu"), sem("act_ready")
        gain_applied, final_row = sem("gain_applied"), [sem("final_row0"), sem("final_row1")]
        dve_step = sem("dve_step")

        class Steps:

            def __init__(self, eng, semaphore, base=0):
                self.eng, self.semaphore, self.base, self.n = eng, semaphore, base, 0

            def __call__(self, ins):
                self.n += 1
                ins.then_inc(self.semaphore, 1)
                self.eng.wait_ge(self.semaphore, self.base + self.n)

        blocks4 = lambda ap: ap.rearrange("p (k t) -> p k t", k=4)
        wide = lambda ap, n: ap.unsqueeze(2).broadcast_to([ap.shape[0], ap.shape[1], n])
        again = lambda ap, n: ap.unsqueeze(1).broadcast_to([ap.shape[0], n, ap.shape[1]])

        def token_part(tile_, c, t, h):
            return tile_[:, 4 * c:4 * c + 4, h, t * P:(t + 1) * P]

        def load(sp, base, j, src, n):
            if not (isinstance(base, int) and base + j < RING):
                sp.wait_ge(lo_ready, base + (j - RING + 1))
            k = src.shape[1]
            dst = stage[:, j % RING, 0:k * n].rearrange("p (k n) -> p k n", n=n)
            sp.dma_start(dst, src).then_inc(staged[j % RING], 16)

        def round_unit(act, quads, j, size=UNIT):
            act.wait_ge(staged[j % RING], quads * 16 + (j // RING + 1) * 16)
            if not (isinstance(quads, int) and 4 * quads + j < RING):
                act.wait_ge(unit_used, quads * 4 + (j - RING + 1))
            act.activation(w_hi[:, j % RING, 0:size], stage[:, j % RING, 0:size], ACT.Copy).then_inc(hi_ready, 1)

        def rest_unit(dve, base, j, size=UNIT):
            dve.wait_ge(hi_ready, base + (j + 1))
            dve.tensor_tensor(w_lo[:, j % RING, 0:size], stage[:, j % RING, 0:size],
                              w_hi[:, j % RING, 0:size].bitcast(F32), ALU.subtract).then_inc(lo_ready, 1)

        def layer_unit_size(j):
            return UNIT // 2 if j in (64, 65) else UNIT

        def product_rows(pe, base, j, lhs, k0, nk, n, pair, first, last):
            pe.wait_ge(lo_ready, base + (j + 1))
            slot = j % RING
            hi = w_hi[:, slot, 0:nk * n].rearrange("p (k n) -> p k n", n=n)
            lo = w_lo[:, slot, 0:nk * n].rearrange("p (k n) -> p k n", n=n)
            for k in range(nk):
                for t in range(T):
                    o = acc[:, 2 * pair + t, 0:n]
                    x_hi = lhs[:, k0 + k, 0, t * P:(t + 1) * P]
                    x_lo = lhs[:, k0 + k, 1, t * P:(t + 1) * P]
                    pe.matmul(o, x_hi, hi[:, k, :], start=first and k == 0, stop=False)
                    pe.matmul(o, x_hi, lo[:, k, :], start=False, stop=False)
                    mm = pe.matmul(o, x_lo, hi[:, k, :], start=False, stop=last and k == nk - 1)
            mm.then_inc(unit_used, 1)

        def product_cols(pe, base, j, k0, pair, first, last):
            pe.wait_ge(lo_ready, base + (j + 1))
            slot = j % RING
            hi = w_hi[:, slot, :].rearrange("p (k n) -> p k n", n=256)
            lo = w_lo[:, slot, :].rearrange("p (k n) -> p k n", n=256)
            for k in range(4):
                both = xT[:, k0 + k, :, :].rearrange("p h t -> p (h t)")
                for c in range(2):
                    o = acc[:, 2 * pair + c, :]
                    cols = slice(c * P, (c + 1) * P)
                    if first and k == 0:
                        pe.matmul(o, hi[:, k, cols], both, start=True, stop=False)
                        mm = pe.matmul(o[:, 0:SEQ], lo[:, k, cols], xT[:, k0 + k, 0, :], start=False, stop=False)
                    else:
                        pe.matmul(o[:, 0:SEQ], lo[:, k, cols], xT[:, k0 + k, 0, :], start=False, stop=False)
                        mm = pe.matmul(o, hi[:, k, cols], both, start=False, stop=last and k == 3)
            mm.then_inc(unit_used, 1)

        def banks_free(pe, pairs, c):
            if not (isinstance(pairs, int) and pairs * 2 + c < 2):
                pe.wait_ge(acc_free[c % 2], pairs + c // 2)

        def evacuated(eng, pairs, c):
            eng.wait_ge(acc_free[c % 2], pairs + (c // 2 + 1))

        def multiplied(eng, base, j):
            eng.wait_ge(unit_used, base + (j + 1))

        def evacuate_scaled(dve, base, j, pair, n, dst, scale):
            multiplied(dve, base, j)
            for t in range(T):
                ins = dve.tensor_scalar(dst(t), acc[:, 2 * pair + t, 0:n], scale[:, t:t + 1], None, ALU.mult)
            ins.then_inc(acc_free[pair], 1)

        def add_to_x(dve, base, j, pair, c):
            multiplied(dve, base, j)
            for t in range(T):
                cols = x[:, t, c * 512:(c + 1) * 512]
                ins = dve.tensor_tensor(cols, acc[:, 2 * pair + t, :], cols, ALU.add)
            ins.then_inc(acc_free[pair], 1)

        def turn(pe, use, src, bank=0, ahead=0):
            if not (isinstance(use, int) and use <= ahead):
                pe.wait_ge(tb_free, use - ahead)
            for i in range(4):
                mm = pe.transpose(aux[:, bank, i * P:(i + 1) * P], src(i), ident[:, :])
            mm.then_inc(tb_filled, 1)

        def x_block(c, t):
            return lambda i: x[:, t, (4 * c + i) * P:(4 * c + i + 1) * P]

        def turn_scale(dve, use, split, gains, slot=0, bank=0):
            dve.wait_ge(tb_filled, use + 1)
            if not (isinstance(split, int) and split <= 0):
                dve.wait_ge(turn_lo, split)
            dve.tensor_tensor(blocks4(turn_f32[:, slot, :]), blocks4(aux[:, bank, :]), wide(gains, P), ALU.mult)\
               .then_inc(tb_free, 1)

        def turn_round(act, use, dst, slot=0):
            act.wait_ge(tb_free, use + 1)
            act.activation(dst, blocks4(turn_f32[:, slot, :]), ACT.Copy).then_inc(turn_hi, 1)

        def turn_rest(dve, turned, dst_hi, dst_lo, slot=0):
            dve.wait_ge(turn_hi, turned + 1)
            dve.tensor_tensor(dst_lo, blocks4(turn_f32[:, slot, :]), dst_hi.bitcast(F32), ALU.subtract)\
               .then_inc(turn_lo, 1)

        def turn_round_plain(act, use, dst, gain):
            act.wait_ge(tb_filled, use + 1)
            act.activation(dst, blocks4(tb), ACT.Copy, scale=gain).then_inc(turn_hi, 1)

        def turn_rest_plain(dve, turned, dst_hi, dst_lo, gain):
            dve.wait_ge(turn_hi, turned + 1)
            dve.scalar_tensor_tensor(out=dst_lo, in0=blocks4(tb), scalar=gain, in1=dst_hi.bitcast(F32),
                                     op0=ALU.mult, op1=ALU.subtract).then_inc(tb_free, 1)

        def rsqrt(step, dve, y, s, n, mean_of, done=None):
            v, t = newton_v[:, 0:n], newton_t[:, 0:n]
            step(dve.tensor_scalar(v, s, 1.0 / mean_of, EPS, ALU.mult, ALU.add))
            step(dve.tensor_scalar(y.bitcast(I32), v.bitcast(I32), -0.5, 1597463007.0, ALU.mult, ALU.add))
            for i in range(3):
                step(dve.tensor_tensor(t, y, y, ALU.mult))
                step(dve.scalar_tensor_tensor(out=t, in0=t, scalar=-0.5, in1=v, op0=ALU.mult, op1=ALU.mult))
                last = dve.scalar_tensor_tensor(out=y, in0=t, scalar=1.5, in1=y, op0=ALU.add, op1=ALU.mult)
                if i == 2 and done is not None:
                    last.then_inc(done, 1)
                else:
                    step(last)

        def x_rstd(step, dve, squares):
            dve.wait_ge(x_squared, squares)
            step(dve.tensor_reduce(sumsq2[:, :], sumsq_x[:, :, :], AX_X, ALU.add))
            rsqrt(step, dve, rstd[:, :], sumsq2[:, :], T, D)

        def square_x(step, act, c):
            for t in range(T):
                step(act.activation(junk[:, :], x[:, t, c * 512:(c + 1) * 512], ACT.Square,
                                    accum_out=sumsq_x[:, t, c:c + 1]))

        mixing = ExitStack()
        mT = sb("mT", [P, KT, 2, SEQ], F32R, mixing)
        bias = sb("bias", [P, HEADS, SEQ], F32, mixing)
        gain_mid = bias[:, :, :].rearrange("p h k -> p (h k)")
        block1 = ExitStack()
        b1 = lambda name, shape, dt=F32: sb(name, shape, dt, block1)
        qa = b1("qa", [P, T, WIDTH])
        kz = b1("kz", [P, T, 2 * WIDTH])
        kr = b1("kr", [P, T, ROPE])
        qb = b1("qb", [P, T, UQ_WIDTH])
        kvb = b1("kvb", [P, T, UKV_WIDTH])
        causal = b1("causal", [P, P])
        rope = b1("rope", [P, T, 2 * ROPE])
        subln_l = b1("subln_l", [P, 1])
        qrT = b1("qrT", [P, HEADS // 2, SEQ])
        krT = b1("krT", [P, SEQ])
        s = b1("s", [P, 3 * SEQ])
        pT = b1("pT", [P, 3 * P])
        neg_lam = b1("neg_lam", [P, LAYERS])
        lam_l = b1("lam_l", [P, 1])
        gain_c = b1("gain_c", [P, 8])
        neg_max = b1("neg_max", [P, 4])
        row_sum = b1("row_sum", [P, 4])
        inv_sum = b1("inv_sum", [P, 4])
        mix_f = b1("mix_f", [P, 2])
        sumsq_o = b1("sumsq_o", [P, HEADS * T])
        rstd_o = b1("rstd_o", [P, HEADS * T])
        sumsq_c = b1("sumsq_c", [P, 4])
        rstd_c = b1("rstd_c", [P, 4])
        sumsq_m = b1("sumsq_m", [P, T, 4])
        sumsq_m2 = b1("sumsq_m2", [P, T])
        rstd_m = b1("rstd_m", [P, T])
        dots = b1("dots", [P, 2 * LAYERS])
        qr = kz[:, :, 0:HEADS * ROPE]
        kr2 = kz[:, :, 512:512 + 2 * ROPE]
        rope_tmp = kz[:, :, 640:640 + HEADS * ROPE // 2]
        mem = kz
        mem_kv1 = qa
        bias_up = kvb[:, 0, :].rearrange("p (h k) -> p h k", h=HEADS)
        lam_raw = kvb[:, 1, 0:LAYERS * 4 * DQ].rearrange("p (l j d) -> p l j d", l=LAYERS, j=4)
        flip = kvb[:, 1, 512:640]
        onehot = kvb[0:BUCKETS, 1, 640:1024]
        table = kvb[0:BUCKETS, 1, 1024:1032]
        future = kvb[0:HEADS, 1, 1032:1416]
        bias_e = kvb[0:HEADS, 1, 1416:1800]
        dot_tmp = kvb[:, 1, 1800:1864]
        par_rows = qb[0:G_ROWS, 0, 0:P]
        ffn_rows = qb[0:FFN_ROWS, 0, P:P + (TAPS + 1) * P]
        fin_rows = qb[0:KT, 0, (TAPS + 2) * P:(TAPS + 3) * P]
        block1.close()

        block2 = ExitStack()
        b2 = lambda name, shape, dt=F32: sb(name, shape, dt, block2)
        half2 = b2("half2", [P, 2, SEQ])
        sum2 = b2("sum2", [P, 2, SEQ])
        rb2 = b2("rb2", [P, T, P])
        rstd_mid = b2("rstd_mid", [P, T])
        rbc2 = b2("rbc2", [P, SEQ])
        zT = b2("zT", [P, 28, SEQ])
        mkv = b2("mkv", [P, T, 2 * D_XATT])
        mkT = b2("mkT", [P, XHEADS, SEQ])
        pool_w = b2("pool_w", [P, N_PIECES, GROUP])
        pool_c = b2("pool_c", [P, CT + CT * 16])
        pool_f = b2("pool_f", [P, 2, SEQ])
        xe = b2("xe", [P, 2, T, SEQ])
        xpT = b2("xpT", [P, T, SEQ])
        xmax = b2("xmax", [P, XHEADS, T])
        xsum = b2("xsum", [P, XHEADS, T])
        xinv = b2("xinv", [P, XHEADS, T])
        block2.close()
        mixing.close()

        ffn_tmp = sb("ffn_tmp", [P, 4, 2, SEQ])
        half3, sum3, gate, value = (ffn_tmp[:, i, :, :] for i in range(4))
        gfin = ffn_tmp[:, :, :, :].rearrange("p a c t -> p (a c t)")
        rb3 = sb("rb3", [P, T, P])
        rbc3 = sb("rbc3", [P, SEQ])
        taps = sb("taps", [P, TAPS + 1, 2, 2])
        act_T = sb("act_T", [P, FT, 2, SEQ], F32R)

        U2 = U_MEM + LAYERS * U_LAYER
        U3 = U2 + U_MIX + U_OUT
        U4 = U3 + N_FFN * U_FFN
        PAIRS2 = (C_MEM + LAYERS * C_LAYER) // 2
        PAIRS3 = PAIRS2 + (14 + 4) // 2
        PAIRS4 = PAIRS3 + N_FFN
        TB2 = TB_PRO + LAYERS * TB_LAYER
        TB3 = TB2 + 2 + 2 + 6
        GAIN2 = TURNS_PRO + LAYERS * GAIN_LAYER
        GAIN3 = GAIN2 + 2 + 6
        TURN2 = TURNS_PRO + LAYERS * TURN_LAYER
        TURN3 = TURN2 + 2 + 6
        SQ_PRO = 8

        with nc.Block() as block:
            @block.sync
            def _(sp):
                for c in range(4):
                    cols = slice(c * 512, (c + 1) * 512)
                    sp.dma_start(mem[:, :, cols], by_token(dram["mem_2"])[:, :, cols]).then_inc(mem_loaded, 16)
                for j in range(4):
                    load(sp, 0, j, w_kv2[:, 2 * j:2 * j + 2, 0:512], 512)
                sp.dma_start(x[:, :, :], by_token(dram["x"])).then_inc(x_loaded, 16)
                for j in range(4, U_MEM):
                    c, k = j // 8, 2 * (j % 8)
                    load(sp, 0, j, w_kv2[:, k:k + 2, c * 512:(c + 1) * 512], 512)
                with sp.Fori(0, LAYERS) as layer:
                    base = layer * U_LAYER + U_MEM

                    def rows(w, tiles, i, nk, c0, n=512):
                        return w[:, bass.ds(layer * tiles + nk * i, nk), c0 if not isinstance(c0, int)
                                 else slice(c0, c0 + n)]

                    for c in range(2):
                        for i in range(8):
                            load(sp, base, 8 * c + i, rows(w_in, KT, i, 2, c * 512), 512)
                    with sp.Fori(0, 2) as half:
                        for c in range(2):
                            for i in range(8):
                                load(sp, base + half * 16, 16 + 8 * c + i,
                                     rows(w_in, KT, i, 2, bass.ds(half * WIDTH + (COL_K + c * 512), 512)), 512)
                    for c in range(2):
                        for i in range(8):
                            load(sp, base, 48 + 8 * c + i, rows(w_in, KT, i, 2, COL_CQ + c * 512), 512)
                    for i in range(2):
                        load(sp, base, 64 + i, rows(w_in, KT, i, 8, COL_KR, ROPE), ROPE)
                    for c in range(3):
                        for i in range(2):
                            load(sp, base, 66 + 2 * c + i, rows(w_uq, 4, i, 2, c * 512), 512)
                    for c in range(4):
                        for i in range(2):
                            load(sp, base, 72 + 2 * c + i, rows(w_ukv, 4, i, 2, c * 512), 512)
                    for c in range(4):
                        for i in range(8):
                            load(sp, base, 80 + 8 * c + i,
                                 rows(w_in, KT, i, 2, (COL_ZA if c < 2 else COL_ZB) + (c % 2) * 512), 512)
                    for c in range(4):
                        for i in range(8):
                            load(sp, base, 112 + 8 * c + i, rows(w_out, KT, i, 2, c * 512), 512)
                for n, tile_ in enumerate(MIX_TILES):
                    for i in range(4):
                        load(sp, U2, 4 * n + i, w_in2[:, 4 * i:4 * i + 4, tile_ * P:tile_ * P + 256], 256)
                for c in range(4):
                    for i in range(8):
                        load(sp, U2, U_MIX + 8 * c + i, w_out2[:, 2 * i:2 * i + 2, c * 512:(c + 1) * 512], 512)
                with sp.Fori(0, N_FFN) as turn_:
                    for half in range(2):
                        for i in range(4):
                            load(sp, turn_ * U_FFN + U3, 4 * half + i,
                                 w_up2[:, 4 * i:4 * i + 4, bass.ds(turn_ * 256 + half * D_FF, 256)], 256)
                for c in range(4):
                    for i in range(FT // 2):
                        load(sp, U4, (FT // 2) * c + i, w_down2[:, 2 * i:2 * i + 2, c * 512:(c + 1) * 512], 512)
                for t in range(T):
                    sp.wait_ge(final_row[t], 1)
                    sp.dma_start(by_token(out)[:, t, :], x[:, t, :]).then_inc(stored, 16)
                sp.wait_ge(stored, 32)

            @block.gpsimd
            def _(pool):
                pool.dma_start(ident[:, :], dram["c_ident"]).then_inc(ident_loaded, 16)
                pool.dma_start(par_rows, dram["par_rows"]).then_inc(par_loaded, 16)
                pool.dma_start(ffn_rows.rearrange("r (j p) -> r j p", p=P),
                               dram["ffn_rows"].rearrange("j r p -> r j p")).then_inc(par_loaded, 16)
                pool.dma_start(fin_rows, dram["final_norm_g"].rearrange("(k p) -> k p", p=P)).then_inc(par_loaded, 16)
                pool.dma_start(kvb[:, 1, 0:LAYERS * 4 * DQ],
                               dram["diff_lambda"].rearrange("l j d -> (l j d)").partition_broadcast(P))\
                    .then_inc(bias_loaded, 16)
                pool.dma_start(flip, dram["c_flip"]).then_inc(bias_loaded, 16)
                pool.dma_start(onehot, dram["c_onehot"]).then_inc(bias_loaded, 16)
                pool.dma_start(table, dram["rel_bias_table"]).then_inc(bias_loaded, 16)
                pool.dma_start(future, dram["c_future"]).then_inc(bias_loaded, 16)
                pool.dma_start(causal[:, :], dram["c_causal"]).then_inc(consts_loaded, 16)
                pool.dma_start(rope[:, :, :], dram["c_rope"].rearrange("(t p) n -> p t n", p=P))\
                    .then_inc(consts_loaded, 16)
                pool.wait_ge(bias_read, 1)
                pool.dma_start(bias_dram, bias_e).then_inc(bias_out, 16)
                pool.wait_ge(bias_out, 16)
                pool.dma_start(bias_up, bias_rows).then_inc(bias_back, 16)
                pool.wait_ge(acc_free[0], 1)
                pool.wait_ge(acc_free[1], 1)
                pool.dma_start(kv_dram, mem_kv1[:, :, :]).then_inc(kv_out, 16)

                pool.wait_ge(consts_loaded, 32)
                with pool.Fori(0, LAYERS) as layer:
                    pairs = layer * (C_LAYER // 2) + C_MEM // 2
                    step = Steps(pool, pool_step, layer * 19)
                    h2 = ROPE // 2
                    evacuated(pool, pairs, 8)
                    pool.wait_ge(tb_filled, layer * TB_LAYER + (TB_PRO + DIFF_TB[-1] + 1))
                    for t in range(T):
                        cos, sin = rope[:, t, 0:ROPE], rope[:, t, ROPE:2 * ROPE]
                        dst = kr2[:, t, :].rearrange("p (a e) -> p a e", a=2)
                        tmp = rope_tmp[:, t, 0:ROPE].rearrange("p (a e) -> p a e", a=2)
                        src = again(kr[:, t, :], 2)
                        step(pool.tensor_tensor(dst, src, again(cos, 2), ALU.mult))
                        step(pool.tensor_tensor(tmp, src[:, :, h2:ROPE], again(sin[:, 0:h2], 2), ALU.mult))
                        step(pool.tensor_tensor(dst[:, :, 0:h2], dst[:, :, 0:h2], tmp, ALU.add))
                        step(pool.tensor_tensor(tmp, src[:, :, 0:h2], again(sin[:, h2:ROPE], 2), ALU.mult))
                        step(pool.tensor_tensor(dst[:, :, h2:ROPE], dst[:, :, h2:ROPE], tmp, ALU.add))
                    evacuated(pool, pairs, 10)
                    evacuated(pool, pairs, 11)
                    for t in range(T):
                        cos, sin = rope[:, t, 0:ROPE], rope[:, t, ROPE:2 * ROPE]
                        src = qb[:, t, :].rearrange("p (h e) -> p h e", h=HEADS)[:, :, NOPE:NOPE + ROPE]
                        dst = qr[:, t, :].rearrange("p (h e) -> p h e", h=HEADS)
                        tmp = rope_tmp[:, t, :].rearrange("p (h e) -> p h e", h=HEADS)
                        step(pool.tensor_tensor(dst, src, again(cos, HEADS), ALU.mult))
                        step(pool.tensor_tensor(tmp, src[:, :, h2:ROPE], again(sin[:, 0:h2], HEADS), ALU.mult))
                        step(pool.tensor_tensor(dst[:, :, 0:h2], dst[:, :, 0:h2], tmp, ALU.add))
                        step(pool.tensor_tensor(tmp, src[:, :, 0:h2], again(sin[:, h2:ROPE], HEADS), ALU.mult))
                        last = pool.tensor_tensor(dst[:, :, h2:ROPE], dst[:, :, h2:ROPE], tmp, ALU.add)
                        if t == 0:
                            step(last)
                        else:
                            last.then_inc(roped, 1)
                    assert step.n == 19
                pool.wait_ge(row_max, (2 * LAYERS - 1) * HEADS)
                pool.dma_start(gain_mid, dram["final_norm_g"].partition_broadcast(P)).then_inc(gmid_loaded, 16)
                evacuated(pool, PAIRS2, -2)
                evacuated(pool, PAIRS2, -1)
                pool.dma_start(mkv[:, :, :], kv_dram).then_inc(mix_loaded, 16)
                pool.dma_start(pool_c[:, :], dram["c_pool"]).then_inc(mix_loaded, 16)
                for i, (_, p0, n) in enumerate(sum(POOL_PIECES, [])):
                    if n < P:
                        pool.memset(pool_w[P - p0 - n:P - p0, i, :], 0.0).then_inc(pool_zeroed, 1)
                w_rows = dram["pool_w_2"].rearrange("l g c d -> (l g c) d")
                for i, (tile_, p0, n) in enumerate(sum(POOL_PIECES, [])):
                    pool.dma_start(pool_w[p0:p0 + n, i, :], w_rows[tile_ * P + p0:tile_ * P + p0 + n, :])\
                        .then_inc(mix_loaded, 16)
                pool.wait_ge(act_ready, N_FFN)
                pool.dma_start(gfin[:, :], dram["g_final_2"].partition_broadcast(P)).then_inc(gfin_loaded, 16)

            @block.tensor
            def _(pe):
                pe.wait_ge(ident_loaded, 16)
                pe.wait_ge(par_loaded, 48)
                pe.transpose(acc[:, 2, 0:G_ROWS], par_rows, ident[0:G_ROWS, 0:G_ROWS])
                pe.transpose(acc[:, 2, G_FIN:G_ALL], fin_rows, ident[0:KT, 0:KT])
                for i in range(TAPS + 1):
                    mm = pe.transpose(acc[:, 3, i * P:i * P + FFN_ROWS], ffn_rows[:, i * P:(i + 1) * P],
                                      ident[0:FFN_ROWS, 0:FFN_ROWS])
                mm.then_inc(par_filled, 1)
                for g in range(8):
                    c, t = g // 2, g % 2
                    pe.wait_ge(mem_loaded, 16 * 4)
                    turn(pe, g, lambda i: mem[:, t, (4 * c + i) * P:(4 * c + i + 1) * P], g % 4, 3)
                pe.wait_ge(bias_loaded, 80)
                pe.matmul(acc[0:HEADS, 0, 0:SEQ + P], table, onehot, start=True, stop=True).then_inc(bias_filled, 1)
                pe.wait_ge(x_loaded, 16)
                for g in range(6):
                    turn(pe, 8 + g, x_block(g // 2, g % 2), g % 4, 3)
                pe.wait_ge(turn_lo, 8)
                pe.wait_ge(par_read, 1)
                pe.wait_ge(bias_read, 1)
                for j in range(U_MEM):
                    c, i = j // 8, j % 8
                    product_rows(pe, 0, j, mT, 2 * i, 2, 512, c, i == 0, i == 7)
                    if j == 7:
                        pe.wait_ge(bias_back, 16)
                        pe.wait_ge(tb_free, TURNS_PRO)
                        for i in range(4):
                            mm = pe.matmul(aux[:, i, :], flip, kvb[:, 0, i * 512:(i + 1) * 512], start=True, stop=True)
                        mm.then_inc(tb_filled, 1)

                with pe.Fori(0, LAYERS) as layer:
                    base = layer * U_LAYER + U_MEM
                    pairs = layer * (C_LAYER // 2) + C_MEM // 2
                    tb0 = layer * TB_LAYER + TB_PRO
                    gain0 = layer * GAIN_LAYER + TURNS_PRO
                    pv0 = layer * (4 * HEADS)
                    head0 = layer * (2 * HEADS)

                    def turn_weights(n, cols):
                        if n > 0:
                            pe.wait_ge(pv_free, pv0 + n)
                        for i, col in enumerate(cols):
                            mm = pe.transpose(pv[:, i * P:(i + 1) * P], s[:, col:col + P], ident[:, :])
                        mm.then_inc(pv_filled, 1)

                    def outputs(n, val):
                        pe.wait_ge(pv_free, pv0 + n)
                        pe.matmul(pv[:, 0:P], pT[:, 0:P], val(0), start=True, stop=False)
                        pe.matmul(pv[:, 0:P], pT[:, P:2 * P], val(1), start=False, stop=True)
                        pe.matmul(pv[:, P:2 * P], pT[:, 2 * P:3 * P], val(0), start=True, stop=True)\
                            .then_inc(pv_filled, 1)

                    def diff_scores(h):
                        pe.wait_ge(tb_free, tb0 + (DIFF_TB[h] + 1))
                        if h > 0:
                            pe.wait_ge(row_max, head0 + h)
                        for col, q, keys in ((0, 1, SEQ), (SEQ, 0, P)):
                            for m, bank in ((0, sc1), (1, sc0)):
                                e = slice(m * DQ, (m + 1) * DQ)
                                mm = pe.matmul(bank[:, col:col + keys], qkT[e, q * P:(q + 1) * P],
                                               qkT[e, 2 * P:2 * P + keys], start=True, stop=True)
                        mm.then_inc(scores_ready, 1)

                    def diff_turn_weights(h):
                        pe.wait_ge(probs_ready, layer * HEADS + (h + 1))
                        turn_weights(2 * h, (0, P, 2 * SEQ))

                    def diff_outputs(h):
                        outputs(2 * h + 1, lambda k: kz[:, k, WIDTH + h * DV:WIDTH + (h + 1) * DV])

                    def mla_scores(h):
                        pe.wait_ge(tb_free, tb0 + (MLA_TB[h] + 1))
                        pe.wait_ge(row_max, head0 + (HEADS + h))
                        e = slice((h % 2) * ROPE, (h % 2 + 1) * ROPE)
                        for col, q, keys in ((0, 1, SEQ), (SEQ, 0, P)):
                            o = sc1[:, col:col + keys]
                            pe.matmul(o, qkT[:, q * P:(q + 1) * P], qkT[:, 2 * P:2 * P + keys], start=True, stop=False)
                            mm = pe.matmul(o, qrT[e, h // 2, q * P:(q + 1) * P], krT[e, 0:keys],
                                           start=False, stop=True)
                        mm.then_inc(scores_ready, 1)

                    def mla_turn_weights(h):
                        pe.wait_ge(rsum_ready, layer * HEADS + (h + 1))
                        turn_weights(2 * HEADS + 2 * h, (0, P, SEQ))

                    def mla_outputs(h):
                        v = h * (NOPE + DV) + NOPE
                        outputs(2 * HEADS + 2 * h + 1, lambda k: kvb[:, k, v:v + DV])

                    def diff_block(h):
                        return lambda i: (qa if i < 2 else kz)[:, i % 2, h * DV:(h + 1) * DV]

                    def mla_block(h):
                        def block_(i):
                            if i < 2:
                                return qb[:, i, h * (NOPE + ROPE):h * (NOPE + ROPE) + NOPE]
                            return kvb[:, i - 2, h * (NOPE + DV):h * (NOPE + DV) + NOPE]
                        return block_

                    def gated_block(g, t):
                        if g < 2:
                            return lambda i: qa[:, t, (4 * g + i) * DV:(4 * g + i + 1) * DV]
                        v = lambda i: (4 * (g - 2) + i) * (NOPE + DV)
                        return lambda i: kvb[:, t, v(i):v(i) + DV]

                    def z_heads(u):
                        h, r = (u - 2) // 4, (u - 2) % 4
                        if u >= 2 and r == 0:
                            if 0 < h <= HEADS:
                                mla_turn_weights(h - 1)
                            if h < HEADS:
                                turn(pe, tb0 + MLA_TB[h], mla_block(h))
                        if u >= 2 and r == 1:
                            if 0 < h <= HEADS:
                                mla_outputs(h - 1)
                            if h < HEADS:
                                mla_scores(h)
                        if u in GATE_TURN:
                            g, t, use = GATE_TURN[u]
                            pe.wait_ge(gated, layer * 8 + (2 * g + t + 1))
                            turn(pe, tb0 + use, gated_block(g, t))

                    for c in range(2):
                        banks_free(pe, pairs, c)
                        for i in range(8):
                            if c == 0 and i in (0, 6):
                                pe.wait_ge(turn_lo, gain0 + (2 if i else 0))
                            product_rows(pe, base, 8 * c + i, xT, 2 * i, 2, 512, c, i == 0, i == 7)
                            if c == 0 and i in (2, 3):
                                evacuated(pe, pairs, -1)
                                turn(pe, tb0 + (i - 2), x_block(3, i - 2))
                    with pe.Fori(0, 2) as half:
                        for c in range(2):
                            banks_free(pe, pairs + half, 2 + c)
                            for i in range(8):
                                product_rows(pe, base + half * 16, 16 + 8 * c + i, xT, 2 * i, 2, 512, c, i == 0, i == 7)
                    for u in range(32):
                        if u < 18:
                            c, i, last_i = u // 8, u % 8, 7 if u < 16 else 1
                        else:
                            c, i, last_i = 3 + (u - 18) // 2, u % 2, 1
                        if i == 0:
                            banks_free(pe, pairs, 6 + c)
                        if u in (18, 24):
                            pe.wait_ge(turn_lo, gain0 + (4 if u == 18 else 6))
                        if u < 16:
                            product_rows(pe, base, 48 + u, xT, 2 * i, 2, 512, c % 2, i == 0, i == last_i)
                        elif u < 18:
                            product_rows(pe, base, 48 + u, xT, 8 * i, 8, ROPE, c % 2, i == 0, i == last_i)
                        else:
                            product_rows(pe, base, 48 + u, mT, (0 if u < 24 else 4) + 2 * i, 2, 512, c % 2,
                                         i == 0, i == last_i)
                        h, r = u // 4, u % 4
                        if u == 0:
                            evacuated(pe, pairs, 4)
                            evacuated(pe, pairs, 5)
                        if r == 0:
                            if h > 0:
                                diff_turn_weights(h - 1)
                            turn(pe, tb0 + DIFF_TB[h], diff_block(h))
                        if r == 1:
                            if h > 0:
                                diff_outputs(h - 1)
                            diff_scores(h)
                        if u in C_TURN:
                            j, t, use = C_TURN[u]
                            evacuated(pe, pairs, 6 + j)
                            turn(pe, tb0 + use, lambda i: qb[:, t, j * RANK + i * P:j * RANK + (i + 1) * P])
                    for u in range(32):
                        c, i = u // 8, u % 8
                        if i == 0:
                            banks_free(pe, pairs, 16 + c)
                        product_rows(pe, base, 80 + u, xT, 2 * i, 2, 512, c % 2, i == 0, i == 7)
                        if u == 0:
                            diff_turn_weights(HEADS - 1)
                            pe.wait_ge(roped, layer + 1)
                            turn(pe, tb0 + QR_TB, lambda i: qr[:, i % 2, (i // 2) * P:(i // 2 + 1) * P])
                        if u == 1:
                            diff_outputs(HEADS - 1)
                            turn(pe, tb0 + (QR_TB + 1), lambda i: qr[:, i % 2, (2 + i // 2) * P:(3 + i // 2) * P])
                            pe.wait_ge(tb_free, tb0 + KR_TB)
                            for t in range(T):
                                mm = pe.transpose(tb[:, t * P:(t + 1) * P], kr2[:, t, :], ident[:, :])
                            mm.then_inc(tb_filled, 1)
                        z_heads(u)
                    for u in range(32):
                        c, i = u // 8, u % 8
                        if i == 0:
                            banks_free(pe, pairs, 20 + c)
                        if u in (0, 6):
                            pe.wait_ge(tb_free, tb0 + (30 if u == 0 else 33))
                        product_rows(pe, base, 112 + u, mT, 2 * i, 2, 512, c % 2, i == 0, i == 7)
                        if u < 8:
                            z_heads(32 + u)
                        if c > 0 and i in (2, 3):
                            evacuated(pe, pairs, 20 + c - 1)
                            turn(pe, tb0 + (X_TB + 2 * (c - 1) + i - 2), x_block(c - 1, i - 2))

                def x_last_chunk(tb_first, pairs_now, t):
                    evacuated(pe, pairs_now, -1)
                    turn(pe, tb_first + t, x_block(3, t))

                def spread_rstd(rb, n):
                    pe.wait_ge(rb_ready, n)
                    for t in range(T):
                        mm = pe.matmul(sc0[:, t * P:(t + 1) * P], rb[:, t, :], ident[:, :], start=True, stop=True)
                    mm.then_inc(rb_filled, 1)

                def pool_matmul(g):
                    if g == 0:
                        pe.wait_ge(pooled_ready, 1)
                        pe.wait_ge(pool_zeroed, 4)
                        pe.wait_ge(tb_free, TB2 + 4)
                    if g == 2:
                        pe.wait_ge(pool_scaled, 1)
                    bank = pv if g == 1 else tb
                    for group, pieces in enumerate(POOL_PIECES):
                        first_channel = 0
                        for tile_, p0, n in pieces:
                            if tile_ // 2 == g:
                                col = (tile_ % 2) * SEQ
                                for k, (kt, _, _) in enumerate(pieces):
                                    mm = pe.matmul(bank[p0:p0 + n, col:col + SEQ],
                                                   pool_w[:, 2 * group + k, first_channel:first_channel + n],
                                                   zT[:, 6 + kt, :],
                                                   start=k == 0, stop=k == len(pieces) - 1)
                            first_channel += n
                    mm.then_inc(pool_filled, 1)

                def cross_heads(u):
                    for h in range(XHEADS):
                        sc = sc1 if h % 2 == 0 else sc0
                        if u == X_SCORE[h]:
                            pe.wait_ge(queries_ready, 1 + h // 2)
                            if h == 0:
                                pe.wait_ge(tb_free, TB2 + 4)
                            if h >= 2:
                                pe.wait_ge(xexp_done, h - 1)
                            for t in range(T):
                                mm = pe.matmul(sc[:, t * SEQ:(t + 1) * SEQ], zT[:, 24 + h, t * P:(t + 1) * P],
                                               mkT[:, h, :], start=True, stop=True)
                            mm.then_inc(xs_ready, 1)
                        if u == X_TURN[h]:
                            pe.wait_ge(xprob_ready, h + 1)
                            if h == 0:
                                pe.wait_ge(pool_scaled, 2)
                            else:
                                pe.wait_ge(xo_lo, h)
                            for k in range(T):
                                for t in range(T):
                                    mm = pe.transpose(pv[:, k * SEQ + t * P:k * SEQ + (t + 1) * P],
                                                      xe[:, h % 2, t, k * P:(k + 1) * P], ident[:, :])
                            mm.then_inc(xpt_filled, 1)
                        if u == X_OUT[h]:
                            pe.wait_ge(xpt_ready, h + 1)
                            v = D_XATT + h * P
                            for k in range(T):
                                mm = pe.matmul(pv[:, 0:SEQ], mkv[:, k, v:v + P], xpT[:, k, :],
                                               start=k == 0, stop=k == T - 1)
                            mm.then_inc(xo_filled, 1)

                for u in range(U_MIX):
                    n, i = u // 4, u % 4
                    if i == 0:
                        banks_free(pe, PAIRS2, n)
                    if u in (0, 3):
                        pe.wait_ge(turn_lo, GAIN2 + (2 if u else 0))
                    product_cols(pe, U2, u, 4 * i, n % 2, i == 0, i == 3)
                    if u in (0, 1):
                        x_last_chunk(TB2, PAIRS2, u)
                    if u == 9:
                        spread_rstd(rb2, 1)
                    if u in (10, 11):
                        pe.wait_ge(mix_loaded, 16 * (2 + N_PIECES))
                        g = u - 10
                        turn(pe, TB2 + 2 + g, lambda i: mkv[:, i % 2, (2 * g + i // 2) * P:(2 * g + i // 2 + 1) * P])
                    if u in POOL_OUT:
                        pool_matmul(u - POOL_OUT[0])
                    cross_heads(u)
                for u in range(U_OUT):
                    c, i = u // 8, u % 8
                    if i == 0:
                        banks_free(pe, PAIRS2, 14 + c)
                    if c == 0:
                        if i < 3:
                            pe.wait_ge(conv_lo, i + 1)
                        elif i < 6:
                            pe.wait_ge(pool_lo, i - 2)
                        else:
                            pe.wait_ge(xo_lo, 2 * (i - 5))
                    product_rows(pe, U2, U_MIX + u, mT, 2 * i, 2, 512, c % 2, i == 0, i == 7)
                    cross_heads(U_MIX + u)
                    if c > 0 and i in (2, 3):
                        if c == 1 and i == 2:
                            pe.wait_ge(pool_scaled, CT // 2)
                        evacuated(pe, PAIRS2, 14 + c - 1)
                        turn(pe, TB2 + 4 + 2 * (c - 1) + i - 2, x_block(c - 1, i - 2))
                def ffn_turn(turn_):
                    first = isinstance(turn_, int)
                    for half in range(2):
                        banks_free(pe, turn_ + PAIRS3, half)
                        for i in range(4):
                            if first and half == 0 and i in (0, 3):
                                pe.wait_ge(turn_lo, GAIN3 + (2 if i else 0))
                            product_cols(pe, turn_ * U_FFN + U3, 4 * half + i, 4 * i, half, i == 0, i == 3)
                            if first and half == 0 and i in (0, 1):
                                x_last_chunk(TB3, PAIRS3, i)
                            if first and half == 0 and i == 2:
                                spread_rstd(rb3, 2)

                ffn_turn(0)
                with pe.Fori(1, N_FFN) as turn_:
                    ffn_turn(turn_)
                for c in range(4):
                    banks_free(pe, PAIRS4, c)
                    for i in range(FT // 2):
                        if c == 0:
                            pe.wait_ge(act_ready, i + 1)
                        product_rows(pe, U4, (FT // 2) * c + i, act_T, 2 * i, 2, 512, c % 2, i == 0, i == FT // 2 - 1)

            @block.scalar
            def _(act):
                for g in range(8):
                    turn_round(act, g, token_part(mT, g // 2, g % 2, 0), g % 2)
                for j in range(LEAD):
                    round_unit(act, 0, j)
                for g in range(6):
                    turn_round(act, 8 + g, token_part(xT, g // 2, g % 2, 0), g % 2)
                step = Steps(act, m_squared)
                for c in range(4):
                    for t in range(T):
                        step(act.activation(junk[:, :], mem[:, t, c * 512:(c + 1) * 512], ACT.Square,
                                            accum_out=sumsq_m[:, t, c:c + 1]))
                act.wait_ge(dots_ready, 1)
                act.activation(dots[:, :], dots[:, :], ACT.Exp).then_inc(exp_dots, 1)
                step = Steps(act, x_squared)
                for j in range(U_MEM):
                    round_unit(act, 0, j + LEAD)
                    if j in (0, 2, 4, 6):
                        square_x(step, act, j // 2)

                with act.Fori(0, LAYERS) as layer:
                    quads = layer * (U_LAYER // RING) + U_MEM // RING
                    pairs = layer * (C_LAYER // 2) + C_MEM // 2
                    tb0 = layer * TB_LAYER + TB_PRO
                    pv0 = layer * (4 * HEADS)
                    head0 = layer * (2 * HEADS)
                    c_step = Steps(act, c_squared, layer * 4)
                    o_step = Steps(act, o_squared, layer * (2 * HEADS))
                    x_step = Steps(act, x_squared, layer * SQ_PRO + SQ_PRO)

                    def rounded(j):
                        round_unit(act, quads, j + LEAD, layer_unit_size(j + LEAD))

                    def copy_bank(use, dst, n=4):
                        act.wait_ge(tb_filled, tb0 + (use + 1))
                        act.activation(dst, tb[:, 0:n * P], ACT.Copy).then_inc(tb_free, 1)

                    def exps(h, parts):
                        act.wait_ge(row_max, head0 + (h + 1))
                        for col, n, r in parts:
                            ins = act.activation(s[:, col:col + n], s[:, col:col + n], ACT.Exp,
                                                 bias=neg_max[:, r:r + 1], accum_out=row_sum[:, r:r + 1])
                        ins.then_inc(exps_done, 1)

                    def copy_weights(n):
                        act.wait_ge(pv_filled, pv0 + (n + 1))
                        act.activation(pT[:, :], pv[:, 0:3 * P], ACT.Copy).then_inc(pv_free, 1)

                    def diff_output(h):
                        act.wait_ge(pv_filled, pv0 + (2 * h + 2))
                        for t, col, r in ((1, 0, 0), (0, P, 2)):
                            o_step(act.activation(junk[:, 0:P], pv[:, col:col + P], ACT.Square,
                                                  scale=inv_sum[:, r:r + 1],
                                                  accum_out=sumsq_o[:, T * h + t:T * h + t + 1]))
                        for t, col, r in ((1, 0, 0), (0, P, 2)):
                            ins = act.activation(qa[:, t, h * DV:(h + 1) * DV], pv[:, col:col + P], ACT.Copy,
                                                 scale=inv_sum[:, r:r + 1])
                        ins.then_inc(pv_free, 1)

                    def mla_output(h):
                        act.wait_ge(pv_filled, pv0 + (2 * HEADS + 2 * h + 2))
                        v = h * (NOPE + DV)
                        for t, col, r in ((1, 0, 0), (0, P, 1)):
                            ins = act.activation(kvb[:, t, v:v + DV], pv[:, col:col + P], ACT.Copy,
                                                 scale=inv_sum[:, r:r + 1])
                        ins.then_inc(pv_free, 1)

                    def z_heads(u):
                        h, r = (u - 2) // 4, (u - 2) % 4
                        if u >= 2 and r == 0:
                            if 0 < h <= HEADS:
                                copy_weights(2 * HEADS + 2 * (h - 1))
                            if h < HEADS:
                                copy_bank(MLA_TB[h], qkT)
                        if u >= 2 and r == 1 and 0 < h <= HEADS:
                            mla_output(h - 1)
                        if u >= 2 and r == 2 and h < HEADS:
                            exps(HEADS + h, ((0, SEQ, 0), (SEQ, P, 1)))
                        if u % 8 == 7 and u < 32:
                            c = u // 8
                            evacuated(act, pairs, 16 + c)
                            z = kz[:, :, c * 512:(c + 1) * 512]
                            act.activation(z, z, ACT.Silu).then_inc(z_silu, 1)
                        if u in GATE_TURN:
                            g, t, use = GATE_TURN[u]
                            turn_round_plain(act, tb0 + use, token_part(mT, g, t, 0),
                                             subln_l[:, 0:1] if g < 2 else 1.0)

                    for j in range(16):
                        rounded(j)
                        if j in (2, 3):
                            turn_round(act, tb0 + (j - 2), token_part(xT, 3, j - 2, 0))
                    with act.Fori(0, 2) as half:
                        for j in range(16):
                            round_unit(act, quads + half * 4, 16 + j + LEAD)
                    for u in range(32):
                        rounded(48 + u)
                        h, r = u // 4, u % 4
                        if r == 0:
                            if h > 0:
                                copy_weights(2 * (h - 1))
                            copy_bank(DIFF_TB[h], qkT)
                        if r == 1 and h > 0:
                            diff_output(h - 1)
                        if r == 2:
                            exps(h, ((0, SEQ, 0), (SEQ, SEQ, 1), (2 * SEQ, P, 2), (2 * SEQ + P, P, 3)))
                        if u in (7, 15):
                            j = u // 8
                            evacuated(act, pairs, 6 + j)
                            for t in range(T):
                                c_step(act.activation(junk[:, :], qb[:, t, j * RANK:(j + 1) * RANK], ACT.Square,
                                                      accum_out=sumsq_c[:, T * j + t:T * j + t + 1]))
                        if u in C_TURN:
                            j, t, use = C_TURN[u]
                            turn_round(act, tb0 + use, token_part(mT, j, t, 0))
                        if u >= 19 and u % 2 == 1:
                            c = (u - 19) // 2
                            act.wait_ge(c_rstd, layer + 1)
                            multiplied(act, quads * 4, 48 + u)
                            for t in range(T):
                                r = (0 if c < 3 else T) + t
                                dst = qb[:, t, c * 512:(c + 1) * 512] if c < 3 else \
                                    kvb[:, t, (c - 3) * 512:(c - 2) * 512]
                                ins = act.activation(dst, acc[:, 2 * ((9 + c) % 2) + t, :], ACT.Copy,
                                                     scale=rstd_c[:, r:r + 1])
                            ins.then_inc(acc_free[(9 + c) % 2], 1)
                    for u in range(32):
                        rounded(80 + u)
                        if u == 0:
                            copy_weights(2 * (HEADS - 1))
                            copy_bank(QR_TB, qrT[:, 0:2, :].rearrange("p a k -> p (a k)"))
                        if u == 1:
                            diff_output(HEADS - 1)
                            copy_bank(QR_TB + 1, qrT[:, 2:4, :].rearrange("p a k -> p (a k)"))
                            copy_bank(KR_TB, krT[:, :], 2)
                        z_heads(u)
                    for u in range(32):
                        rounded(112 + u)
                        if u < 8:
                            z_heads(32 + u)
                        c, i = u // 8, u % 8
                        if c > 0 and i in (2, 3):
                            turn_round(act, tb0 + (X_TB + 2 * (c - 1) + i - 2), token_part(xT, c - 1, i - 2, 0))
                        if i == 7:
                            evacuated(act, pairs, 20 + c)
                            square_x(x_step, act, c)

                def copy_half(half, base, j, pair, pairs_now, c):
                    multiplied(act, base, j)
                    evacuated(act, pairs_now, c - 1)
                    act.activation(half[:, :, :], acc[:, 2 * pair:2 * pair + 2, SEQ:2 * SEQ], ACT.Copy)\
                       .then_inc(half_copied, 1)

                def cross_heads(u):
                    for h in range(XHEADS):
                        sc = sc1 if h % 2 == 0 else sc0
                        if u == X_SCORE[h] + 1:
                            act.wait_ge(xmax_ready, h + 1)
                            for t in range(T):
                                ins = act.activation(xe[:, h % 2, t, :], sc[:, t * SEQ:(t + 1) * SEQ], ACT.Exp,
                                                     bias=xmax[:, h, t:t + 1], scale=X_SCALE,
                                                     accum_out=xsum[:, h, t:t + 1])
                            ins.then_inc(xexp_done, 1)
                        if u == X_TURN[h]:
                            act.wait_ge(xpt_filled, h + 1)
                            act.activation(xpT[:, :, :].rearrange("p k t -> p (k t)"), pv, ACT.Copy)\
                               .then_inc(xpt_ready, 1)
                        if u == X_OUT[h]:
                            act.wait_ge(xo_filled, h + 1)
                            act.activation(mT[:, 12 + h, 0, :], pv[:, 0:SEQ], ACT.Copy).then_inc(xo_hi, 1)

                quads2 = U2 // RING
                x_step = Steps(act, x_squared, SQ_PRO * (1 + LAYERS))
                for u in range(U_MIX):
                    round_unit(act, quads2, u + LEAD)
                    if 4 <= u < 8:
                        act.wait_ge(x_normed, u - 3)
                        square_x(x_step, act, u - 4)
                    n, i = u // 4, u % 4
                    if u in (0, 1):
                        turn_round(act, TB2 + u, token_part(xT, 3, u, 0))
                    if u in (10, 11):
                        g = u - 10
                        act.wait_ge(tb_filled, TB2 + 3 + g)
                        act.activation(mkT[:, 2 * g:2 * g + 2, :].rearrange("p h k -> p (h k)"), tb,
                                       ACT.Copy).then_inc(tb_free, 1)
                    if i == 3:
                        copy_half(half2, U2, u, n % 2, PAIRS2, n)
                    if i == 0 and 6 < n < 10:
                        g = n - 7
                        act.wait_ge(conv_ready, g + 1)
                        act.activation(mT[:, 2 * g:2 * g + 2, 0, :], zT[:, 12 + 2 * g:14 + 2 * g, :], ACT.Copy)\
                           .then_inc(conv_hi, 1)
                    if u in POOL_OUT:
                        g = u - POOL_OUT[0]
                        act.wait_ge(pool_scaled, g + 1)
                        act.activation(mT[:, 6 + 2 * g:8 + 2 * g, 0, :], pool_f[:, :, :], ACT.Copy).then_inc(pool_hi, 1)
                    cross_heads(u)
                x_step = Steps(act, x_squared, SQ_PRO * (2 + LAYERS))
                for u in range(U_OUT):
                    round_unit(act, quads2, U_MIX + u + LEAD)
                    cross_heads(U_MIX + u)
                    c, i = u // 8, u % 8
                    if c > 0 and i in (2, 3):
                        turn_round(act, TB2 + 4 + 2 * (c - 1) + i - 2, token_part(xT, c - 1, i - 2, 0))
                    if i == 7:
                        evacuated(act, PAIRS2, 14 + c)
                        square_x(x_step, act, c)
                def ffn_turn(turn_):
                    first = isinstance(turn_, int)
                    for half in range(2):
                        for i in range(4):
                            round_unit(act, turn_ * (U_FFN // RING) + U3 // RING, 4 * half + i + LEAD)
                            if first and half == 0 and i in (0, 1):
                                turn_round(act, TB3 + i, token_part(xT, 3, i, 0))
                        copy_half(half3, turn_ * U_FFN + U3, 4 * half + 3, half, turn_ + PAIRS3, half)
                        if half == 0:
                            act.wait_ge(gate_conv, turn_ + 1)
                            act.activation(gate[:, :, :], gate[:, :, :], ACT.Silu).then_inc(gate_silu, 1)

                ffn_turn(0)
                with act.Fori(1, N_FFN) as turn_:
                    ffn_turn(turn_)
                x_step = Steps(act, x_squared, SQ_PRO * (3 + LAYERS))
                for c in range(4):
                    for i in range(FT // 2):
                        j = (FT // 2) * c + i
                        if j + LEAD < U_DOWN:
                            round_unit(act, U4 // RING, j + LEAD)
                    evacuated(act, PAIRS4, c)
                    square_x(x_step, act, c)
                act.wait_ge(gain_applied, 4)
                act.activation(x[:, 1, :], x[:, 1, :], ACT.Copy, scale=rstd[:, 1:2]).then_inc(final_row[1], 1)

            @block.vector
            def _(dve):
                step = Steps(dve, dve_step)
                dve.wait_ge(par_filled, 1)
                dve.tensor_copy(par[:, :], acc[:, 2, 0:G_ALL])
                dve.tensor_copy(par_ffn[:, :, :], acc[:, 3, :].rearrange("p (j r) -> p j r", r=P)[:, :, 0:FFN_ROWS])\
                   .then_inc(par_read, 1)
                dve.wait_ge(par_read, 1)
                for l in range(LAYERS):
                    g = par[:, G_SUBLN + l:G_SUBLN + l + 1]
                    step(dve.tensor_scalar(g, g, 1.0 - lam_init(l), None, ALU.mult))
                step(dve.tensor_tensor(par[:, G_MIX:G_MIX + KT], par[:, G_MIX:G_MIX + KT], par[:, G_FIN:G_ALL], ALU.mult))

                def split_turned(first, n, tile_, gain):
                    for g in range(n + 1):
                        if g < n:
                            k = gain + 4 * (g // 2)
                            turn_scale(dve, first + g, first + g - 1, par[:, k:k + 4], g % 2, (first + g) % 4)
                        if g > 0:
                            c, t = (g - 1) // 2, (g - 1) % 2
                            turn_rest(dve, first + g - 1, token_part(tile_, c, t, 0), token_part(tile_, c, t, 1),
                                      (g - 1) % 2)

                split_turned(0, 8, mT, G_MEM)
                for j in range(LEAD):
                    rest_unit(dve, 0, j)
                dve.wait_ge(bias_filled, 1)
                dve.wait_ge(bias_loaded, 80)
                dve.tensor_tensor(bias_e, acc[0:HEADS, 0, 0:SEQ + P], future, ALU.add).then_inc(bias_read, 1)
                split_turned(8, 6, xT, G_NORM)
                for l in range(LAYERS):
                    for i in range(2):
                        ins = dve.tensor_tensor_reduce(out=dot_tmp, in0=lam_raw[:, l, 2 * i, :],
                                                       in1=lam_raw[:, l, 2 * i + 1, :], scale=1.0, scalar=0.0,
                                                       op0=ALU.mult, op1=ALU.add,
                                                       accum_out=dots[:, 2 * l + i:2 * l + i + 1])
                        if (l, i) == (LAYERS - 1, 1):
                            ins.then_inc(dots_ready, 1)
                        else:
                            step(ins)
                dve.wait_ge(exp_dots, 1)
                for l in range(LAYERS):
                    step(dve.tensor_tensor(neg_lam[:, l:l + 1], dots[:, 2 * l + 1:2 * l + 2], dots[:, 2 * l:2 * l + 1],
                                           ALU.subtract))
                    step(dve.tensor_scalar(neg_lam[:, l:l + 1], neg_lam[:, l:l + 1], -lam_init(l), None, ALU.add))
                for j in range(U_MEM):
                    rest_unit(dve, 0, j + LEAD)
                    if j == 0:
                        dve.wait_ge(m_squared, 8)
                        step(dve.tensor_reduce(sumsq_m2[:, :], sumsq_m[:, :, :], AX_X, ALU.add))
                        rsqrt(step, dve, rstd_m[:, :], sumsq_m2[:, :], T, D)
                    if j in (7, 15):
                        c = j // 8
                        evacuate_scaled(dve, 0, j, c, 512, lambda t: mem_kv1[:, t, c * 512:(c + 1) * 512], rstd_m)
                    if j == 8:
                        dve.wait_ge(tb_filled, TB_PRO)
                        dve.tensor_copy(bias[:, :, :].rearrange("p h k -> p (h k)"),
                                        aux[:, :, :].rearrange("p b k -> p (b k)")).then_inc(tb_free, 1)
                dve.wait_ge(kv_out, 16)
                dve.wait_ge(consts_loaded, 32)
                steps_before = step.n

                with dve.Fori(0, LAYERS) as layer:
                    base = layer * U_LAYER + U_MEM
                    pairs = layer * (C_LAYER // 2) + C_MEM // 2
                    tb0 = layer * TB_LAYER + TB_PRO
                    gain0 = layer * GAIN_LAYER + TURNS_PRO
                    turn0 = layer * TURN_LAYER + TURNS_PRO
                    head0 = layer * (2 * HEADS)
                    step = Steps(dve, dve_step, layer * DVE_STEPS_LAYER + steps_before)

                    def rest(j):
                        rest_unit(dve, base, j + LEAD, layer_unit_size(j + LEAD))

                    def diff_max(h):
                        dve.wait_ge(scores_ready, head0 + (h + 1))
                        two = lambda ap: ap.rearrange("p (m k) -> p m k", m=2)
                        dve.scalar_tensor_tensor(out=two(s[:, 0:2 * SEQ]), in0=aux[:, 1:3, 0:SEQ], scalar=DIFF_SCALE,
                                                 in1=again(bias[:, h, :], 2), op0=ALU.mult, op1=ALU.add)
                        step(dve.scalar_tensor_tensor(out=two(s[:, 2 * SEQ:3 * SEQ]), in0=aux[:, 1:3, SEQ:SEQ + P],
                                                      scalar=DIFF_SCALE, in1=again(bias[:, h, P:SEQ], 2),
                                                      op0=ALU.mult, op1=ALU.add))
                        dve.tensor_reduce(neg_max[:, 0:2], two(s[:, 0:2 * SEQ]), AX_X, ALU.max)
                        step(dve.tensor_reduce(neg_max[:, 2:4], two(s[:, 2 * SEQ:3 * SEQ]), AX_X, ALU.max))
                        dve.tensor_scalar(neg_max[:, :], neg_max[:, :], -1.0, None, ALU.mult).then_inc(row_max, 1)

                    def diff_weights(h):
                        dve.wait_ge(exps_done, head0 + (h + 1))
                        step(dve.reciprocal(inv_sum[:, :], row_sum[:, :]))
                        pairs_of = lambda ap, i: ap[:, :].rearrange("p (t m) -> p t m", m=2)[:, :, i]
                        step(dve.scalar_tensor_tensor(out=mix_f[:, :], in0=pairs_of(row_sum, 0), scalar=lam_l[:, 0:1],
                                                      in1=pairs_of(inv_sum, 1), op0=ALU.mult, op1=ALU.mult))
                        dve.scalar_tensor_tensor(out=s[:, 0:SEQ], in0=s[:, SEQ:2 * SEQ], scalar=mix_f[:, 0:1],
                                                 in1=s[:, 0:SEQ], op0=ALU.mult, op1=ALU.add)
                        dve.scalar_tensor_tensor(out=s[:, 2 * SEQ:2 * SEQ + P], in0=s[:, 2 * SEQ + P:3 * SEQ],
                                                 scalar=mix_f[:, 1:2], in1=s[:, 2 * SEQ:2 * SEQ + P],
                                                 op0=ALU.mult, op1=ALU.add).then_inc(probs_ready, 1)

                    def mla_max(h):
                        dve.wait_ge(scores_ready, head0 + (HEADS + h + 1))
                        dve.tensor_scalar(s[:, 0:P], sc1[:, 0:P], MLA_SCALE, None, ALU.mult)
                        two = lambda ap: ap.rearrange("p (m k) -> p m k", m=2)
                        step(dve.scalar_tensor_tensor(out=two(s[:, P:3 * P]), in0=two(sc1[:, P:3 * P]), scalar=MLA_SCALE,
                                                      in1=again(causal[:, :], 2), op0=ALU.mult, op1=ALU.add))
                        dve.tensor_reduce(neg_max[:, 0:1], s[:, 0:SEQ], AX_X, ALU.max)
                        step(dve.tensor_reduce(neg_max[:, 1:2], s[:, SEQ:SEQ + P], AX_X, ALU.max))
                        dve.tensor_scalar(neg_max[:, 0:2], neg_max[:, 0:2], -1.0, None, ALU.mult).then_inc(row_max, 1)

                    def mla_sums(h):
                        dve.wait_ge(exps_done, head0 + (HEADS + h + 1))
                        dve.reciprocal(inv_sum[:, 0:2], row_sum[:, 0:2]).then_inc(rsum_ready, 1)

                    def gate_outputs(g, t):
                        dve.wait_ge(z_silu, layer * 4 + (g + 1))
                        z = kz[:, t, g * 512:(g + 1) * 512].rearrange("p (h d) -> p h d", h=4)
                        if g < 2:
                            o = qa[:, t, g * 512:(g + 1) * 512].rearrange("p (h d) -> p h d", h=4)
                            r = rstd_o[:, :].rearrange("p (h t) -> p h t", t=T)[:, 4 * g:4 * g + 4, t]
                            step(dve.tensor_tensor(o, o, wide(r, DV), ALU.mult))
                        else:
                            dve.wait_ge(pv_free, layer * (4 * HEADS) + (2 * HEADS + 8 * (g - 1)))
                            o = kvb[:, t, :].rearrange("p (h e) -> p h e", h=HEADS)[:, 4 * (g - 2):4 * (g - 1), 0:DV]
                        dve.tensor_tensor(o, o, z, ALU.mult).then_inc(gated, 1)

                    def z_heads(u):
                        if u >= 3 and (u - 3) % 4 == 0 and (u - 3) // 4 < HEADS:
                            mla_max((u - 3) // 4)
                        if u >= 5 and (u - 5) % 4 == 0 and (u - 5) // 4 < HEADS:
                            mla_sums((u - 5) // 4)
                        if u % 8 == 7 and u < 32:
                            c = u // 8
                            evacuate_scaled(dve, base, 80 + u, c % 2, 512,
                                            lambda t: kz[:, t, c * 512:(c + 1) * 512], rstd)
                        for g, steps_ in enumerate(((9, 10), (17, 18), (25, 26), (35, 35))):
                            for t in range(T):
                                if u == steps_[t]:
                                    gate_outputs(g, t)
                        if u in GATE_TURN:
                            g, t, use = GATE_TURN[u]
                            turn_rest_plain(dve, turn0 + (6 + 2 * g + t), token_part(mT, g, t, 0), token_part(mT, g, t, 1),
                                            subln_l[:, 0:1] if g < 2 else 1.0)

                    step(dve.tensor_scalar(lam_l[:, 0:1], neg_lam[:, bass.ds(layer, 1)], 1.0, None, ALU.mult))
                    step(dve.tensor_scalar(subln_l[:, :], par[:, bass.ds(layer + G_SUBLN, 1)], 1.0, None, ALU.mult))
                    step(dve.tensor_scalar(gain_c[:, 0:4], par[:, bass.ds(layer * 4 + G_Q, 4)], 1.0, None, ALU.mult))
                    step(dve.tensor_scalar(gain_c[:, 4:8], par[:, bass.ds(layer * 4 + G_KV, 4)], 1.0, None, ALU.mult))
                    for j in range(16):
                        rest(j)
                        if j in (2, 3):
                            turn_scale(dve, tb0 + (j - 2), gain0 + (j - 2), par[:, bass.ds(layer * KT + 12, 4)])
                            turn_rest(dve, turn0 + (j - 2), token_part(xT, 3, j - 2, 0), token_part(xT, 3, j - 2, 1))
                        if j == 4:
                            x_rstd(step, dve, layer * SQ_PRO + SQ_PRO)
                        if j in (7, 15):
                            c = j // 8
                            evacuate_scaled(dve, base, j, c, 512, lambda t: qa[:, t, c * 512:(c + 1) * 512], rstd)
                    with dve.Fori(0, 2) as half:
                        for j in range(16):
                            rest_unit(dve, base + half * 16, 16 + j + LEAD)
                            if j in (7, 15):
                                c = j // 8
                                evacuate_scaled(dve, base + half * 16, 16 + j, c, 512,
                                                lambda t: kz[:, t, bass.ds(half * WIDTH + c * 512, 512)], rstd)
                    for u in range(32):
                        rest(48 + u)
                        if u in (7, 15):
                            j = u // 8
                            evacuate_scaled(dve, base, 48 + u, j, 512, lambda t: qb[:, t, j * RANK:(j + 1) * RANK], rstd)
                        if u == 16:
                            dve.wait_ge(c_squared, layer * 4 + 4)
                            rsqrt(step, dve, rstd_c[:, :], sumsq_c[:, :], 4, RANK, done=c_rstd)
                        if u == 17:
                            evacuate_scaled(dve, base, 48 + u, 0, ROPE, lambda t: kr[:, t, :], rstd)
                        if u in C_TURN:
                            j, t, use = C_TURN[u]
                            turn_scale(dve, tb0 + use, gain0 + (2 + 2 * j + t), gain_c[:, 4 * j:4 * j + 4])
                            turn_rest(dve, turn0 + (2 + 2 * j + t), token_part(mT, j, t, 0), token_part(mT, j, t, 1))
                        if u % 4 == 1:
                            diff_max(u // 4)
                        if u % 4 == 3:
                            diff_weights(u // 4)
                    for u in range(32):
                        rest(80 + u)
                        if u == 2:
                            dve.wait_ge(o_squared, layer * (2 * HEADS) + 2 * HEADS)
                            rsqrt(step, dve, rstd_o[:, :], sumsq_o[:, :], HEADS * T, DV)
                        z_heads(u)
                    for u in range(32):
                        rest(112 + u)
                        if u < 8:
                            z_heads(32 + u)
                        c, i = u // 8, u % 8
                        if c > 0 and i in (2, 3):
                            k = 2 * (c - 1) + i - 2
                            turn_scale(dve, tb0 + (X_TB + k), gain0 + (6 + k),
                                       par[:, bass.ds(layer * KT + (KT + 4 * (c - 1)), 4)])
                            turn_rest(dve, turn0 + (14 + k), token_part(xT, c - 1, i - 2, 0),
                                      token_part(xT, c - 1, i - 2, 1))
                        if i == 7:
                            add_to_x(dve, base, 112 + u, c % 2, c)
                    assert step.n == DVE_STEPS_LAYER, step.n
                step = Steps(dve, dve_step, steps_before + LAYERS * DVE_STEPS_LAYER)

                def spread(rb, squares, also=None):
                    x_rstd(step, dve, squares)
                    if also is not None:
                        step(dve.tensor_tensor(rstd[:, :], rstd[:, :], also[:, :], ALU.mult))
                    for t in range(T):
                        ins = dve.tensor_scalar(rb[:, t, :], ident[:, :], 0.0, rstd[:, t:t + 1], ALU.mult, ALU.add)
                    ins.then_inc(rb_ready, 1)

                def spread_read(rbc, n):
                    dve.wait_ge(rb_filled, n)
                    step(dve.tensor_copy(rbc[:, :], sc0[:, 0:SEQ]))

                def both_halves(half, total, pair, copied):
                    dve.wait_ge(half_copied, copied)
                    dve.tensor_tensor(total, acc[:, 2 * pair:2 * pair + 2, 0:SEQ], half[:, :, :], ALU.add)\
                       .then_inc(acc_free[pair], 1)

                def conv_taps(y, u, tap, done=None):
                    if len(tap) > TAPS:
                        step(dve.tensor_scalar(y, u, tap[2], tap[3], ALU.mult, ALU.add))
                    else:
                        step(dve.tensor_scalar(y, u, tap[2], None, ALU.mult))
                    for d in (1, 2):
                        last = dve.scalar_tensor_tensor(out=y[:, d:SEQ], in0=u[:, 0:SEQ - d], scalar=tap[2 - d],
                                                        in1=y[:, d:SEQ], op0=ALU.mult, op1=ALU.add)
                        if d == 2 and done is not None:
                            last.then_inc(done, 1)
                        else:
                            step(last)

                def pool_sums(u):
                    v, s2, s4, s8, s16 = zT[:, 18:24, :], zT[:, 0:6, :], zT[:, 6:12, :], zT[:, 12:18, :], zT[:, 0:6, :]

                    def double(dst, src, first, d):
                        dve.tensor_tensor(dst[:, first:CT, d:SEQ], src[:, first:CT, d:SEQ], src[:, first:CT, 0:SEQ - d],
                                          ALU.add)
                        step(dve.tensor_copy(dst[:, first:CT, 0:d], src[:, first:CT, 0:d]))

                    if u == 48:
                        double(s2, v, 0, 1)
                        double(s4, s2, 1, 2)
                    if u == 49:
                        double(s8, s4, 3, 4)
                        double(s16, s8, 4, 8)
                    if u == 50:
                        for tile_, p0, n, src in ((0, 0, P, s2), (1, 0, 64, s2), (1, 64, 64, s4), (2, 0, P, s4),
                                                  (3, 0, P, s8), (4, 0, 64, s8), (4, 64, 64, s16), (5, 0, P, s16)):
                            e = slice(p0, p0 + n)
                            step(dve.tensor_scalar(s4[e, tile_, :], src[e, tile_, :], pool_c[e, tile_:tile_ + 1], None,
                                                   ALU.mult))
                        early = s4[:, :, 0:16]
                        step(dve.tensor_tensor(early, early, pool_c[:, CT:CT + CT * 16].rearrange("p (t k) -> p t k", k=16),
                                               ALU.mult))
                        dve.tensor_tensor(s4, s4, v, ALU.subtract).then_inc(pooled_ready, 1)

                def cross_heads(u):
                    for h in range(XHEADS):
                        sc = sc1 if h % 2 == 0 else sc0
                        if u == X_SCORE[h]:
                            dve.wait_ge(xs_ready, h + 1)
                            step(dve.tensor_reduce(xmax[:, h, :], sc.rearrange("p (t k) -> p t k", t=T), AX_X, ALU.max))
                            dve.tensor_scalar(xmax[:, h, :], xmax[:, h, :], -X_SCALE, None, ALU.mult)\
                               .then_inc(xmax_ready, 1)
                        if u == X_SCORE[h] + 2:
                            dve.wait_ge(xexp_done, h + 1)
                            step(dve.reciprocal(xinv[:, h, :], xsum[:, h, :]))
                            for t in range(T):
                                e = xe[:, h % 2, t, :]
                                ins = dve.tensor_scalar(e, e, xinv[:, h, t:t + 1], None, ALU.mult)
                            ins.then_inc(xprob_ready, 1)
                        if u == X_OUT[h]:
                            dve.wait_ge(xo_hi, h + 1)
                            dve.tensor_tensor(mT[:, 12 + h, 1, :], pv[:, 0:SEQ], mT[:, 12 + h, 0, :].bitcast(F32),
                                              ALU.subtract).then_inc(xo_lo, 1)

                for u in range(U_MIX):
                    rest_unit(dve, U2, u + LEAD)
                    n, i = u // 4, u % 4
                    if u in (0, 1):
                        turn_scale(dve, TB2 + u, GAIN2 + u, par[:, G_MIX + 12:G_MIX + 16])
                        turn_rest(dve, TURN2 + u, token_part(xT, 3, u, 0), token_part(xT, 3, u, 1))
                    if u == 1:
                        x_rstd(step, dve, SQ_PRO * (1 + LAYERS))
                        step(dve.tensor_copy(rstd_mid[:, :], rstd[:, :]))
                    if 3 <= u < 7:
                        if u == 3:
                            dve.wait_ge(gmid_loaded, 16)
                            dve.wait_ge(tb_filled, TB2 + 2)
                        cols = slice((u - 3) * 512, (u - 2) * 512)
                        for t in range(T):
                            ins = dve.scalar_tensor_tensor(out=x[:, t, cols], in0=x[:, t, cols],
                                                           scalar=rstd_mid[:, t:t + 1], in1=gain_mid[:, cols],
                                                           op0=ALU.mult, op1=ALU.mult)
                        ins.then_inc(x_normed, 1)
                    if u == 8:
                        spread(rb2, SQ_PRO * (2 + LAYERS), rstd_mid)
                    if u == 9:
                        spread_read(rbc2, 1)
                    if i == 3:
                        tile_ = MIX_TILES[n]
                        pair = zT[:, tile_:tile_ + 2, :]
                        both_halves(half2, pair if n < 3 else sum2[:, :, :], n % 2, n + 1)
                        evacuated(dve, PAIRS2, n)
                        if n >= 12:
                            dve.tensor_tensor(pair, sum2[:, :, :], again(rbc2[:, :], 2), ALU.mult)\
                               .then_inc(queries_ready, 1)
                            dve.wait_ge(queries_ready, n - 11)
                        elif n >= 3:
                            step(dve.tensor_tensor(pair, sum2[:, :, :], again(rbc2[:, :], 2), ALU.mult))
                        if 3 <= n < 6:
                            c_pair = zT[:, tile_ - 6:tile_ - 4, :]
                            step(dve.tensor_tensor(c_pair, c_pair, again(rbc2[:, :], 2), ALU.mult))
                            step(dve.tensor_tensor(c_pair, c_pair, pair, ALU.mult))
                        if 6 <= n < 9:
                            for k in range(2):
                                t_ = tile_ + k
                                taps_ = [par[:, G_CONV + j * CT + t_:G_CONV + j * CT + t_ + 1] for j in range(TAPS)]
                                conv_taps(zT[:, 12 + t_, :], zT[:, 6 + t_, :], taps_)
                            y = zT[:, 12 + tile_:14 + tile_, :]
                            dve.tensor_tensor(y, y, pair, ALU.mult).then_inc(conv_ready, 1)
                    if i == 1 and 6 < n < 10:
                        g = n - 7
                        dve.wait_ge(conv_hi, g + 1)
                        dve.tensor_tensor(mT[:, 2 * g:2 * g + 2, 1, :], zT[:, 12 + 2 * g:14 + 2 * g, :],
                                          mT[:, 2 * g:2 * g + 2, 0, :].bitcast(F32), ALU.subtract).then_inc(conv_lo, 1)
                    if u == 48:
                        dve.wait_ge(mix_loaded, 16 * (2 + N_PIECES))
                    pool_sums(u)
                    if u in POOL_OUT:
                        g = u - POOL_OUT[0]
                        dve.wait_ge(pool_filled, g + 1)
                        if g > 0:
                            dve.wait_ge(pool_lo, g)
                        bank = (pv if g == 1 else tb).rearrange("p (c t) -> p c t", c=2)
                        dve.tensor_tensor(pool_f[:, :, :], bank, wide(par[:, G_POOL + 2 * g:G_POOL + 2 * g + 2], SEQ),
                                          ALU.mult).then_inc(pool_scaled, 1)
                        dve.wait_ge(pool_hi, g + 1)
                        dve.tensor_tensor(mT[:, 6 + 2 * g:8 + 2 * g, 1, :], pool_f[:, :, :],
                                          mT[:, 6 + 2 * g:8 + 2 * g, 0, :].bitcast(F32), ALU.subtract).then_inc(pool_lo, 1)
                    cross_heads(u)
                for u in range(U_OUT):
                    rest_unit(dve, U2, U_MIX + u + LEAD)
                    cross_heads(U_MIX + u)
                    c, i = u // 8, u % 8
                    if c > 0 and i in (2, 3):
                        k = 2 * (c - 1) + i - 2
                        g = G_FFN + 4 * (c - 1)
                        turn_scale(dve, TB2 + 4 + k, GAIN2 + 2 + k, par[:, g:g + 4])
                        turn_rest(dve, TURN2 + 2 + k, token_part(xT, c - 1, i - 2, 0), token_part(xT, c - 1, i - 2, 1))
                    if i == 7:
                        add_to_x(dve, U2, U_MIX + u, c % 2, c)
                steps_before_ffn = step.base + step.n
                step.base, step.n = steps_before_ffn, 0

                def ffn_turn(turn_, first):
                    for half in range(2):
                        base = turn_ * U_FFN + U3
                        for i in range(4):
                            rest_unit(dve, base, 4 * half + i + LEAD)
                            if first and half == 0 and i in (0, 1):
                                turn_scale(dve, TB3 + i, GAIN3 + i, par[:, G_FFN + 12:G_FFN + 16])
                                turn_rest(dve, TURN3 + i, token_part(xT, 3, i, 0), token_part(xT, 3, i, 1))
                            if first and half == 0 and i == 1:
                                spread(rb3, SQ_PRO * (3 + LAYERS))
                            if first and half == 0 and i == 2:
                                spread_read(rbc3, 2)
                        if first and half == 0:
                            assert step.n == FIRST_FFN_STEPS, step.n
                            step.base, step.n = steps_before_ffn + FIRST_FFN_STEPS, 0
                        y = value if half else gate
                        step(dve.tensor_scalar(taps[:, :, half, :], par_ffn[:, :, bass.ds(turn_ * 2 + half * FT, 2)],
                                               1.0, None, ALU.mult))
                        both_halves(half3, sum3[:, :, :], half, turn_ * 2 + (14 + half + 1))
                        evacuated(dve, turn_ + PAIRS3, half)
                        step(dve.tensor_tensor(sum3[:, :, :], sum3[:, :, :], again(rbc3[:, :], 2), ALU.mult))
                        for k in range(2):
                            tap = [taps[:, j, half, k:k + 1] for j in range(TAPS + 1)]
                            conv_taps(y[:, k, :], sum3[:, k, :], tap, gate_conv if (half, k) == (0, 1) else None)
                        if half == 0:
                            dve.wait_ge(gate_conv, turn_ + 1)
                    dve.wait_ge(gate_silu, turn_ + 1)
                    step(dve.tensor_tensor(value[:, :, :], value[:, :, :], gate[:, :, :], ALU.mult))
                    hi = act_T[:, bass.ds(turn_ * 2, 2), 0, :]
                    step(dve.tensor_scalar(hi, value[:, :, :], 1.0, None, ALU.mult))
                    dve.tensor_tensor(act_T[:, bass.ds(turn_ * 2, 2), 1, :], value[:, :, :], hi.bitcast(F32),
                                      ALU.subtract).then_inc(act_ready, 1)

                ffn_turn(0, True)
                steps0 = steps_before_ffn + FIRST_FFN_STEPS
                assert step.n == FFN_STEPS, step.n
                with dve.Fori(1, N_FFN) as turn_:
                    step.base, step.n = turn_ * FFN_STEPS + steps0, 0
                    ffn_turn(turn_, False)
                step.base, step.n = steps0 + N_FFN * FFN_STEPS, 0
                dve.wait_ge(gfin_loaded, 16)

                def apply_gain(c):
                    cols = slice(c * 512, (c + 1) * 512)
                    dve.wait_ge(x_squared, SQ_PRO * (3 + LAYERS) + 2 * (c + 1))
                    for t in range(T):
                        ins = dve.tensor_tensor(x[:, t, cols], x[:, t, cols], gfin[:, cols], ALU.mult)
                    ins.then_inc(gain_applied, 1)
                    if c == 3:
                        dve.wait_ge(gain_applied, 4)

                for c in range(4):
                    for i in range(FT // 2):
                        j = (FT // 2) * c + i
                        if j + LEAD < U_DOWN:
                            rest_unit(dve, U4, j + LEAD)
                        if c > 0 and i == 4:
                            apply_gain(c - 1)
                    add_to_x(dve, U4, (FT // 2) * (c + 1) - 1, c % 2, c)
                x_rstd(step, dve, SQ_PRO * (4 + LAYERS))
                apply_gain(3)
                dve.tensor_scalar(x[:, 0, :], x[:, 0, :], rstd[:, 0:1], None, ALU.mult).then_inc(final_row[0], 1)


def kernel(**arrays):
    import concourse.bacc as _bacc
    from concourse.bass_utils import run_bass_kernel_spmd

    rows = lambda name: np.asarray(arrays[name]).reshape(-1, P)
    data = {n: np.asarray(arrays[n]) for n in (
        "x", "w_in", "diff_lambda", "rel_bias_table", "w_uq", "w_ukv", "w_out", "final_norm_g",
        "mem_2", "w_in_2", "pool_w_2", "w_kv_2", "w_out_2", "w_up_2", "w_down_2", "g_final_2")}
    data["par_rows"] = np.concatenate([rows(n) for n in (
        "norm_g", "g_mix_2", "g_ffn_2", "mla_q_norm_g", "mla_kv_norm_g", "pool_scale_2", "conv_w_2", "g_mem_2", "diff_subln_g")])
    data["ffn_rows"] = np.concatenate([rows("ffn_conv_w_2"), rows("ffn_conv_b_2")]).reshape(TAPS + 1, FFN_ROWS, P)
    data.update(shape_constants())

    nc = _bacc.Bacc("TRN2", target_bir_lowering=False, num_devices=1)
    dram = {n: nc.dram_tensor(n, list(a.shape), F32, kind="ExternalInput").ap() for n, a in data.items()}
    out = nc.dram_tensor("out", [1, SEQ, D], F32, kind="ExternalOutput")
    build(nc, dram, out.ap())
    nc.compile()
    r = run_bass_kernel_spmd(nc, [data], core_ids=[0])
    return r.results[0]["out"]
```

```python
import math
from contextlib import ExitStack

import numpy as np

import concourse.bass as bass
from concourse import mybir
from concourse.alu_op_type import AluOpType as ALU

F32 = mybir.dt.float32
F32R = mybir.dt.float32r
BF16 = mybir.dt.bfloat16
I32 = mybir.dt.int32
ACT = mybir.ActivationFunctionType
AX_X = mybir.AxisListType.X

P = 128
SEQ = 256
T = SEQ // P
D = 2048
KT = D // P
LAYERS = 2
EPS = 1e-6
NEG = -1e30

HEADS = 8
DQ = 64
DV = 128
NOPE, ROPE = 128, 64
RANK = 512
WIDTH = HEADS * DV
COL_Q, COL_K, COL_V, COL_ZA = 0, WIDTH, 2 * WIDTH, 3 * WIDTH
COL_CQ = 4 * WIDTH
COL_CKV = COL_CQ + RANK
COL_KR = COL_CKV + RANK
COL_ZB = COL_KR + ROPE
IN_WIDTH = COL_ZB + WIDTH
UQ_WIDTH = HEADS * (NOPE + ROPE)
UKV_WIDTH = HEADS * (NOPE + DV)
DIFF_SCALE = DQ ** -0.5
MLA_SCALE = (NOPE + ROPE) ** -0.5
BUCKETS, MAX_DIST = 32, 128
THETA = 10000.0

D_CONV = 3 * D // 8
D_POOL = D_CONV
D_XATT = D // 4
XHEADS = 4
X_SCALE = (D_XATT // XHEADS) ** -0.5
WINDOWS = (2, 4, 8, 16)
GROUP = D_POOL // len(WINDOWS)
CT = D_CONV // P
D_FF = ((8 * D // 3 + 255) // 256) * 256
FT = D_FF // P
TAPS = 3

UNIT = 1024
RING = 4
LEAD = 3
U_MEM = 16
U_LAYER = 48 + 32 + 32 + 32
U_MIX = 14 * 4
U_OUT = 32
U_FFN = 8
N_FFN = D_FF // 256
U_DOWN = 4 * (FT // 2)
U_ALL = U_MEM + LAYERS * U_LAYER + U_MIX + U_OUT + N_FFN * U_FFN + U_DOWN
C_MEM, C_LAYER = 2, 24

G_NORM = 0
G_MIX = G_NORM + LAYERS * KT
G_FFN = G_MIX + KT
G_Q = G_FFN + KT
G_KV = G_Q + LAYERS * 4
G_POOL = G_KV + LAYERS * 4
G_CONV = G_POOL + CT
G_MEM = G_CONV + TAPS * CT
G_SUBLN = G_MEM + KT
G_ROWS = G_SUBLN + LAYERS
G_FIN = G_ROWS
G_ALL = G_FIN + KT
FFN_ROWS = 2 * FT
assert G_ROWS <= P and FFN_ROWS <= P

TURNS_PRO = 2 * 8 - 2
TB_PRO = TURNS_PRO + 1
TB_LAYER = 38
GAIN_LAYER = 12
TURN_LAYER = 20
DIFF_TB = [2, 3, 4, 7, 8, 11, 12, 13]
C_TURN = {10: (0, 0, 5), 11: (0, 1, 6), 18: (1, 0, 9), 19: (1, 1, 10)}
QR_TB = 14
MLA_TB = [16, 17, 18, 21, 22, 25, 26, 29]
GATE_TURN = {12: (0, 0, 19), 13: (0, 1, 20), 20: (1, 0, 23), 21: (1, 1, 24), 28: (2, 0, 27), 29: (2, 1, 28),
             36: (3, 0, 30), 37: (3, 1, 31)}
X_TB = 32
DVE_STEPS_LAYER = 90
FIRST_FFN_STEPS, FFN_STEPS = 15, 7
X_SCORE = [41, 44, 47, 50]
X_TURN, X_OUT = [u + 3 for u in X_SCORE], [u + 4 for u in X_SCORE]
POOL_SUMS = [50, 54, 57]
POOL_OUT = [55, 59, 60]
MIX_TILES = [6, 8, 10, 12, 14, 16, 0, 2, 4, 24, 26, 18, 20, 22]
N_QUERY, N_POOL = 9, 11
OUT_PAIRS = [0, 1, 2, 6, 7, 3, 4, 5]
POOL_PIECES = [[(0, 0, 128), (1, 0, 64)], [(1, 64, 64), (2, 0, 128)],
               [(3, 0, 128), (4, 0, 64)], [(4, 64, 64), (5, 0, 128)]]
N_PIECES = sum(len(pieces) for pieces in POOL_PIECES)


def lam_init(layer):
    return 0.8 - 0.6 * math.exp(-0.3 * layer)


def shape_constants():
    ident = np.eye(P, dtype=np.float32)
    j = np.arange(SEQ + P)
    dist = SEQ - 1 - j
    n = np.maximum(dist, 0)
    half = BUCKETS // 2
    large = half + (np.log(np.maximum(n, 1) / half) / math.log(MAX_DIST / half) * half + 1e-9).astype(np.int64)
    bucket = np.where(n < half, n, np.minimum(large, BUCKETS - 1))
    onehot = ((bucket[None, :] == np.arange(BUCKETS)[:, None]) & (dist >= 0)[None, :]).astype(np.float32)
    future = np.broadcast_to(np.where(dist < 0, NEG, 0.0), (HEADS, SEQ + P)).astype(np.float32)
    q, k = np.arange(P)[:, None], np.arange(P)[None, :]
    causal = np.where(q - k >= 0, 0.0, NEG).astype(np.float32)
    inv = (1.0 / (THETA ** (np.arange(0, ROPE, 2, dtype=np.float32) / ROPE))).astype(np.float32)
    ang = np.arange(SEQ, dtype=np.float32)[:, None] * inv[None, :]
    rope = np.concatenate([np.cos(ang), np.cos(ang), -np.sin(ang), np.sin(ang)], axis=1)
    window = np.repeat(np.array(WINDOWS), GROUP).reshape(CT, P).T
    count = np.minimum(np.arange(16)[None, None, :] + 1, window[:, :, None])
    pool = np.concatenate([1.0 / window, (window[:, :, None] / count).reshape(P, -1)], axis=1)
    return {
        "c_ident": ident, "c_flip": np.ascontiguousarray(ident[::-1]), "c_onehot": onehot,
        "c_future": np.ascontiguousarray(future), "c_causal": causal,
        "c_rope": np.ascontiguousarray(rope.astype(np.float32)),
        "c_pool": np.ascontiguousarray(pool.astype(np.float32)),
    }


def build(nc, dram, out):
    k_tiled = lambda w: w.rearrange("l (k p) n -> p (l k) n", p=P)
    w_in, w_uq, w_ukv, w_out = (k_tiled(dram[n]) for n in ("w_in", "w_uq", "w_ukv", "w_out"))
    w_kv2, w_in2, w_out2, w_up2, w_down2 = (
        k_tiled(dram[n]) for n in ("w_kv_2", "w_in_2", "w_out_2", "w_up_2", "w_down_2"))
    by_token = lambda a: a.rearrange("b (t p) d -> p (b t) d", p=P)
    bias_dram = nc.dram_tensor("bias_by_distance", [HEADS, SEQ + P], F32, kind="Internal").ap()
    kv_dram = nc.dram_tensor("mem_kv", [P, T, 2 * D_XATT], F32, kind="Internal").ap()
    bias_rows = bass.AP(tensor=bias_dram.tensor, offset=0, ap=[[1, P], [SEQ + P, HEADS], [1, SEQ]])

    ctx = ExitStack()
    with ctx:
        def sb(name, shape, dt=F32, stack=ctx):
            return stack.enter_context(nc.sbuf_tensor("sb_" + name, shape, dt))

        def sem(name):
            return ctx.enter_context(nc.semaphore(name))

        stage = sb("stage", [P, RING, UNIT])
        w_hi = sb("w_hi", [P, RING, UNIT], F32R)
        w_lo = sb("w_lo", [P, RING, UNIT], F32R)
        x = sb("x", [P, T, D])
        xT = sb("xT", [P, KT, 2, SEQ], F32R)
        ident = sb("ident", [P, P])
        par = sb("par", [P, G_ALL])
        par_ffn = sb("par_ffn", [P, TAPS + 1, FFN_ROWS])
        turn_f32 = sb("turn_f32", [P, 2, 512])
        qkT = turn_f32[:, 1, :]
        sumsq_x = sb("sumsq_x", [P, T, 4])
        sumsq2 = sb("sumsq2", [P, T])
        rstd = sb("rstd", [P, T])
        newton_v = sb("newton_v", [P, 16])
        newton_t = sb("newton_t", [P, 16])
        junk = sb("junk", [P, 512], BF16)

        acc = ctx.enter_context(nc.psum_tensor("acc", [P, 4, 512], F32))
        aux = ctx.enter_context(nc.psum_tensor("aux", [P, 4, 512], F32))
        tb = aux[:, 0, :]
        sc1, sc0 = aux[:, 1, :], aux[:, 2, :]
        pv = aux[:, 3, :]

        staged = [sem(f"staged{i}") for i in range(RING)]
        hi_ready = sem("hi_ready")
        lo_ready = sem("lo_ready")
        unit_used = sem("unit_used")
        acc_free = [sem("acc_free0"), sem("acc_free1")]
        tb_filled, tb_free = sem("tb_filled"), sem("tb_free")
        turn_hi, turn_lo = sem("turn_hi"), sem("turn_lo")
        par_loaded, rows_loaded = sem("par_loaded"), sem("rows_loaded")
        x_loaded = [sem(f"x_loaded{c}") for c in range(4)]
        mem_loaded = [sem(f"mem_loaded{c}") for c in range(4)]
        ident_loaded, bias_loaded, consts_loaded = sem("ident_loaded"), sem("bias_loaded"), sem("consts_loaded")
        bias_out, bias_back, kv_out = sem("bias_out"), sem("bias_back"), sem("kv_out")
        mix_loaded, gfin_loaded, stored = sem("mix_loaded"), sem("gfin_loaded"), sem("stored")
        gmid_loaded = sem("gmid_loaded")
        par_filled, par_read = sem("par_filled"), sem("par_read")
        bias_filled, bias_read = sem("bias_filled"), sem("bias_read")
        dots_ready, exp_dots = sem("dots_ready"), sem("exp_dots")
        m_squared = sem("m_squared")
        x_squared, c_squared, o_squared = sem("x_squared"), sem("c_squared"), sem("o_squared")
        c_rstd = sem("c_rstd")
        key_summed, key_turned = sem("key_summed"), sem("key_turned")
        x_normed = sem("x_normed")
        roped, pool_step = sem("roped"), sem("pool_step")
        scores_ready, row_max, exps_done = sem("scores_ready"), sem("row_max"), sem("exps_done")
        probs_ready, rsum_ready = sem("probs_ready"), sem("rsum_ready")
        pv_filled, pv_free = sem("pv_filled"), sem("pv_free")
        z_silu, gated = sem("z_silu"), sem("gated")
        rb_ready, rb_filled = sem("rb_ready"), sem("rb_filled")
        half_copied = sem("half_copied")
        conv_ready, conv_hi, conv_lo = sem("conv_ready"), sem("conv_hi"), sem("conv_lo")
        pool_zeroed = sem("pool_zeroed")
        pooled_ready, pool_filled, pool_scaled = sem("pooled_ready"), sem("pool_filled"), sem("pool_scaled")
        pool_hi, pool_lo = sem("pool_hi"), sem("pool_lo")
        queries_ready = sem("queries_ready")
        xs_ready, xmax_ready, xexp_done, xprob_ready = (
            sem("xs_ready"), sem("xmax_ready"), sem("xexp_done"), sem("xprob_ready"))
        xpt_filled, xpt_ready, xo_filled = sem("xpt_filled"), sem("xpt_ready"), sem("xo_filled")
        xo_hi, xo_lo = sem("xo_hi"), sem("xo_lo")
        sum_ready, tap2_done = sem("sum_ready"), sem("tap2_done")
        gate_conv, gate_silu, act_ready = sem("gate_conv"), sem("gate_silu"), sem("act_ready")
        last_added, final_rstd = sem("last_added"), sem("final_rstd")
        final_last = [sem("final_last0"), sem("final_last1")]
        gain_applied, final_row = sem("gain_applied"), [sem("final_row0"), sem("final_row1")]
        dve_step = sem("dve_step")

        class Steps:

            def __init__(self, eng, semaphore, base=0):
                self.eng, self.semaphore, self.base, self.n = eng, semaphore, base, 0

            def __call__(self, ins):
                self.n += 1
                ins.then_inc(self.semaphore, 1)
                self.eng.wait_ge(self.semaphore, self.base + self.n)

        blocks4 = lambda ap: ap.rearrange("p (k t) -> p k t", k=4)
        wide = lambda ap, n: ap.unsqueeze(2).broadcast_to([ap.shape[0], ap.shape[1], n])
        again = lambda ap, n: ap.unsqueeze(1).broadcast_to([ap.shape[0], n, ap.shape[1]])

        def token_part(tile_, c, t, h):
            return tile_[:, 4 * c:4 * c + 4, h, t * P:(t + 1) * P]

        def load(sp, base, j, src, n):
            if not (isinstance(base, int) and base + j < RING):
                sp.wait_ge(lo_ready, base + (j - RING + 1))
            k = src.shape[1]
            dst = stage[:, j % RING, 0:k * n].rearrange("p (k n) -> p k n", n=n)
            sp.dma_start(dst, src).then_inc(staged[j % RING], 16)

        def round_unit(act, quads, j, size=UNIT):
            act.wait_ge(staged[j % RING], quads * 16 + (j // RING + 1) * 16)
            if not (isinstance(quads, int) and 4 * quads + j < RING):
                act.wait_ge(unit_used, quads * 4 + (j - RING + 1))
            act.activation(w_hi[:, j % RING, 0:size], stage[:, j % RING, 0:size], ACT.Copy).then_inc(hi_ready, 1)

        def rest_unit(dve, base, j, size=UNIT):
            dve.wait_ge(hi_ready, base + (j + 1))
            dve.tensor_tensor(w_lo[:, j % RING, 0:size], stage[:, j % RING, 0:size],
                              w_hi[:, j % RING, 0:size].bitcast(F32), ALU.subtract).then_inc(lo_ready, 1)

        def layer_unit_size(j):
            return UNIT // 2 if j in (64, 65) else UNIT

        def product_rows(pe, base, j, lhs, k0, nk, n, pair, first, last, before_tile1=None):
            pe.wait_ge(lo_ready, base + (j + 1))
            slot = j % RING
            hi = w_hi[:, slot, 0:nk * n].rearrange("p (k n) -> p k n", n=n)
            lo = w_lo[:, slot, 0:nk * n].rearrange("p (k n) -> p k n", n=n)
            k_outer = [(k, t) for k in range(nk) for t in range(T)]
            t_outer = [(k, t) for t in range(T) for k in range(nk)]
            for k, t in t_outer if before_tile1 else k_outer:
                if before_tile1 and (k, t) == (0, 1):
                    before_tile1()
                o = acc[:, 2 * pair + t, 0:n]
                x_hi = lhs[:, k0 + k, 0, t * P:(t + 1) * P]
                x_lo = lhs[:, k0 + k, 1, t * P:(t + 1) * P]
                pe.matmul(o, x_hi, hi[:, k, :], start=first and k == 0, stop=False)
                pe.matmul(o, x_hi, lo[:, k, :], start=False, stop=False)
                mm = pe.matmul(o, x_lo, hi[:, k, :], start=False, stop=last and k == nk - 1)
            mm.then_inc(unit_used, 1)

        def product_cols(pe, base, j, k0, pair, first, last):
            pe.wait_ge(lo_ready, base + (j + 1))
            slot = j % RING
            hi = w_hi[:, slot, :].rearrange("p (k n) -> p k n", n=256)
            lo = w_lo[:, slot, :].rearrange("p (k n) -> p k n", n=256)
            for k in range(4):
                both = xT[:, k0 + k, :, :].rearrange("p h t -> p (h t)")
                for c in range(2):
                    o = acc[:, 2 * pair + c, :]
                    cols = slice(c * P, (c + 1) * P)
                    if first and k == 0:
                        pe.matmul(o, hi[:, k, cols], both, start=True, stop=False)
                        mm = pe.matmul(o[:, 0:SEQ], lo[:, k, cols], xT[:, k0 + k, 0, :], start=False, stop=False)
                    else:
                        pe.matmul(o[:, 0:SEQ], lo[:, k, cols], xT[:, k0 + k, 0, :], start=False, stop=False)
                        mm = pe.matmul(o, hi[:, k, cols], both, start=False, stop=last and k == 3)
            mm.then_inc(unit_used, 1)

        def product_rope_key(pe, base, j, k0, first, last):
            pe.wait_ge(lo_ready, base + (j + 1))
            slot = j % RING
            hi = w_hi[:, slot, 0:8 * ROPE].rearrange("p (k n) -> p k n", n=ROPE)
            lo = w_lo[:, slot, 0:8 * ROPE].rearrange("p (k n) -> p k n", n=ROPE)
            o = acc[0:ROPE, 0, :]
            for k in range(8):
                both = xT[:, k0 + k, :, :].rearrange("p h t -> p (h t)")
                if not (first and k == 0):
                    pe.matmul(o[:, 0:SEQ], lo[:, k, :], xT[:, k0 + k, 0, :], start=False, stop=False)
                mm = pe.matmul(o, hi[:, k, :], both, start=first and k == 0, stop=last and k == 7)
                if first and k == 0:
                    mm = pe.matmul(o[:, 0:SEQ], lo[:, k, :], xT[:, k0 + k, 0, :], start=False, stop=False)
            mm.then_inc(unit_used, 1)

        def banks_free(pe, pairs, c):
            if not (isinstance(pairs, int) and pairs * 2 + c < 2):
                pe.wait_ge(acc_free[c % 2], pairs + c // 2)

        def evacuated(eng, pairs, c):
            eng.wait_ge(acc_free[c % 2], pairs + (c // 2 + 1))

        def multiplied(eng, base, j):
            eng.wait_ge(unit_used, base + (j + 1))

        def evacuate_scaled(dve, base, j, pair, n, dst, scale):
            multiplied(dve, base, j)
            for t in range(T):
                ins = dve.tensor_scalar(dst(t), acc[:, 2 * pair + t, 0:n], scale[:, t:t + 1], None, ALU.mult)
            ins.then_inc(acc_free[pair], 1)

        def add_to_x(dve, base, j, pair, c):
            multiplied(dve, base, j)
            for t in range(T):
                cols = x[:, t, c * 512:(c + 1) * 512]
                ins = dve.tensor_tensor(cols, acc[:, 2 * pair + t, :], cols, ALU.add)
            ins.then_inc(acc_free[pair], 1)

        def turn(pe, use, src, bank=0, ahead=0):
            if not (isinstance(use, int) and use <= ahead):
                pe.wait_ge(tb_free, use - ahead)
            for i in range(4):
                mm = pe.transpose(aux[:, bank, i * P:(i + 1) * P], src(i), ident[:, :])
            mm.then_inc(tb_filled, 1)

        def x_block(c, t):
            return lambda i: x[:, t, (4 * c + i) * P:(4 * c + i + 1) * P]

        def turn_scale(dve, use, split, gains, slot=0, bank=0):
            dve.wait_ge(tb_filled, use + 1)
            if not (isinstance(split, int) and split <= 0):
                dve.wait_ge(turn_lo, split)
            dve.tensor_tensor(blocks4(turn_f32[:, slot, :]), blocks4(aux[:, bank, :]), wide(gains, P), ALU.mult)\
               .then_inc(tb_free, 1)

        def turn_round(act, use, dst, slot=0):
            act.wait_ge(tb_free, use + 1)
            act.activation(dst, blocks4(turn_f32[:, slot, :]), ACT.Copy).then_inc(turn_hi, 1)

        def turn_rest(dve, turned, dst_hi, dst_lo, slot=0):
            dve.wait_ge(turn_hi, turned + 1)
            dve.tensor_tensor(dst_lo, blocks4(turn_f32[:, slot, :]), dst_hi.bitcast(F32), ALU.subtract)\
               .then_inc(turn_lo, 1)

        def turn_round_plain(act, use, dst, gain):
            act.wait_ge(tb_filled, use + 1)
            act.activation(dst, blocks4(tb), ACT.Copy, scale=gain).then_inc(turn_hi, 1)

        def turn_rest_plain(dve, turned, dst_hi, dst_lo, gain):
            dve.wait_ge(turn_hi, turned + 1)
            dve.scalar_tensor_tensor(out=dst_lo, in0=blocks4(tb), scalar=gain, in1=dst_hi.bitcast(F32),
                                     op0=ALU.mult, op1=ALU.subtract).then_inc(tb_free, 1)

        def rsqrt(step, dve, y, s, n, mean_of, done=None):
            v, t = newton_v[:, 0:n], newton_t[:, 0:n]
            step(dve.tensor_scalar(v, s, 1.0 / mean_of, EPS, ALU.mult, ALU.add))
            step(dve.tensor_scalar(y.bitcast(I32), v.bitcast(I32), -0.5, 1597463007.0, ALU.mult, ALU.add))
            for i in range(3):
                step(dve.tensor_tensor(t, y, y, ALU.mult))
                step(dve.scalar_tensor_tensor(out=t, in0=t, scalar=-0.5, in1=v, op0=ALU.mult, op1=ALU.mult))
                last = dve.scalar_tensor_tensor(out=y, in0=t, scalar=1.5, in1=y, op0=ALU.add, op1=ALU.mult)
                if i == 2 and done is not None:
                    last.then_inc(done, 1)
                else:
                    step(last)

        def x_rstd(step, dve, squares, done=None):
            dve.wait_ge(x_squared, squares)
            step(dve.tensor_reduce(sumsq2[:, :], sumsq_x[:, :, :], AX_X, ALU.add))
            rsqrt(step, dve, rstd[:, :], sumsq2[:, :], T, D, done)

        def square_x(step, act, c, tiles=range(T)):
            for t in tiles:
                step(act.activation(junk[:, :], x[:, t, c * 512:(c + 1) * 512], ACT.Square,
                                    accum_out=sumsq_x[:, t, c:c + 1]))

        mixing = ExitStack()
        mT = sb("mT", [P, KT, 2, SEQ], F32R, mixing)
        bias = sb("bias", [P, HEADS, SEQ], F32, mixing)
        gain_mid = bias[:, :, :].rearrange("p h k -> p (h k)")
        block1 = ExitStack()
        b1 = lambda name, shape, dt=F32: sb(name, shape, dt, block1)
        qa = b1("qa", [P, T, WIDTH])
        kz = b1("kz", [P, T, 2 * WIDTH])
        kr = b1("kr", [P, T, ROPE])
        qb = b1("qb", [P, T, UQ_WIDTH])
        kvb = b1("kvb", [P, T, UKV_WIDTH])
        causal = b1("causal", [P, P])
        rope = b1("rope", [P, T, 2 * ROPE])
        subln_l = b1("subln_l", [P, 1])
        qrT = b1("qrT", [P, HEADS // 2, SEQ])
        krT = b1("krT", [P, SEQ])
        s = b1("s", [P, 3 * SEQ])
        pT = b1("pT", [P, 3 * P])
        neg_lam = b1("neg_lam", [P, LAYERS])
        lam_l = b1("lam_l", [P, 1])
        gain_c = b1("gain_c", [P, 8])
        neg_max = b1("neg_max", [P, 4])
        row_sum = b1("row_sum", [P, 4])
        inv_sum = b1("inv_sum", [P, 4])
        mix_f = b1("mix_f", [P, 2])
        sumsq_o = b1("sumsq_o", [P, HEADS * T])
        rstd_o = b1("rstd_o", [P, HEADS * T])
        sumsq_c = b1("sumsq_c", [P, 4])
        rstd_c = b1("rstd_c", [P, 4])
        sumsq_m = b1("sumsq_m", [P, T, 4])
        sumsq_m2 = b1("sumsq_m2", [P, T])
        rstd_m = b1("rstd_m", [P, T])
        dots = b1("dots", [P, 2 * LAYERS])
        qr = kz[:, :, 0:HEADS * ROPE]
        kr2 = kz[:, :, 512:512 + 2 * ROPE]
        rope_tmp = kz[:, :, 640:640 + HEADS * ROPE // 2]
        mem = kz
        mem_kv1 = qa
        bias_up = kvb[:, 0, :].rearrange("p (h k) -> p h k", h=HEADS)
        lam_raw = kvb[:, 1, 0:LAYERS * 4 * DQ].rearrange("p (l j d) -> p l j d", l=LAYERS, j=4)
        flip = kvb[:, 1, 512:640]
        onehot = kvb[0:BUCKETS, 1, 640:1024]
        table = kvb[0:BUCKETS, 1, 1024:1032]
        future = kvb[0:HEADS, 1, 1032:1416]
        bias_e = kvb[0:HEADS, 1, 1416:1800]
        dot_tmp = kvb[:, 1, 1800:1864]
        par_rows = qb[0:G_ROWS, 0, 0:P]
        ffn_rows = qb[0:FFN_ROWS, 0, P:P + (TAPS + 1) * P]
        fin_rows = qb[0:KT, 0, (TAPS + 2) * P:(TAPS + 3) * P]
        block1.close()

        block2 = ExitStack()
        b2 = lambda name, shape, dt=F32: sb(name, shape, dt, block2)
        half2 = b2("half2", [P, 2, SEQ])
        sum2 = b2("sum2", [P, 2, SEQ])
        rb2 = b2("rb2", [P, T, P])
        rstd_mid = b2("rstd_mid", [P, T])
        rbc2 = b2("rbc2", [P, SEQ])
        zT = b2("zT", [P, 28, SEQ])
        mkv = b2("mkv", [P, T, 2 * D_XATT])
        mkT = b2("mkT", [P, XHEADS, SEQ])
        pool_w = b2("pool_w", [P, N_PIECES, GROUP])
        pool_c = b2("pool_c", [P, CT + CT * 16])
        pool_f = b2("pool_f", [P, 2, SEQ])
        xe = b2("xe", [P, 2, T, SEQ])
        xpT = b2("xpT", [P, T, SEQ])
        xmax = b2("xmax", [P, XHEADS, T])
        xsum = b2("xsum", [P, XHEADS, T])
        xinv = b2("xinv", [P, XHEADS, T])
        block2.close()
        mixing.close()

        ffn_tmp = sb("ffn_tmp", [P, 4, 2, SEQ])
        half3, sum3, gate, value = (ffn_tmp[:, i, :, :] for i in range(4))
        gfin = ffn_tmp[:, :, :, :].rearrange("p a c t -> p (a c t)")
        rb3 = sb("rb3", [P, T, P])
        rbc3 = sb("rbc3", [P, SEQ])
        taps = sb("taps", [P, TAPS + 1, 2, 2])
        act_T = sb("act_T", [P, FT, 2, SEQ], F32R)

        U2 = U_MEM + LAYERS * U_LAYER
        U3 = U2 + U_MIX + U_OUT
        U4 = U3 + N_FFN * U_FFN
        PAIRS2 = (C_MEM + LAYERS * C_LAYER) // 2
        PAIRS3 = PAIRS2 + (14 + 4) // 2
        PAIRS4 = PAIRS3 + N_FFN
        TB2 = TB_PRO + LAYERS * TB_LAYER
        TB3 = TB2 + 2 + 2 + 6
        GAIN2 = TURNS_PRO + LAYERS * GAIN_LAYER
        GAIN3 = GAIN2 + 2 + 6
        TURN2 = TURNS_PRO + LAYERS * TURN_LAYER
        TURN3 = TURN2 + 2 + 6
        SQ_PRO = 8

        with nc.Block() as block:
            @block.sync
            def _(sp):
                sp.dma_start(ident[:, :], dram["c_ident"]).then_inc(ident_loaded, 16)
                sp.dma_start(par_rows, dram["par_rows"]).then_inc(par_loaded, 16)
                for c in range(4):
                    cols = slice(c * 512, (c + 1) * 512)
                    sp.dma_start(mem[:, :, cols], by_token(dram["mem_2"])[:, :, cols]).then_inc(mem_loaded[c], 16)
                    load(sp, 0, c, w_kv2[:, 2 * c:2 * c + 2, 0:512], 512)
                for j in range(4, U_MEM):
                    c, k = j // 8, 2 * (j % 8)
                    load(sp, 0, j, w_kv2[:, k:k + 2, c * 512:(c + 1) * 512], 512)
                    if j < 8:
                        cols = slice((j - 4) * 512, (j - 3) * 512)
                        sp.dma_start(x[:, :, cols], by_token(dram["x"])[:, :, cols]).then_inc(x_loaded[j - 4], 16)
                with sp.Fori(0, LAYERS) as layer:
                    base = layer * U_LAYER + U_MEM

                    def rows(w, tiles, i, nk, c0, n=512):
                        return w[:, bass.ds(layer * tiles + nk * i, nk), c0 if not isinstance(c0, int)
                                 else slice(c0, c0 + n)]

                    for c in range(2):
                        for i in range(8):
                            load(sp, base, 8 * c + i, rows(w_in, KT, i, 2, c * 512), 512)
                    with sp.Fori(0, 2) as half:
                        for c in range(2):
                            for i in range(8):
                                load(sp, base + half * 16, 16 + 8 * c + i,
                                     rows(w_in, KT, i, 2, bass.ds(half * WIDTH + (COL_K + c * 512), 512)), 512)
                    for c in range(2):
                        for i in range(8):
                            load(sp, base, 48 + 8 * c + i, rows(w_in, KT, i, 2, COL_CQ + c * 512), 512)
                    for i in range(2):
                        load(sp, base, 64 + i, rows(w_in, KT, i, 8, COL_KR, ROPE), ROPE)
                    for c in range(3):
                        for i in range(2):
                            load(sp, base, 66 + 2 * c + i, rows(w_uq, 4, i, 2, c * 512), 512)
                    for c in range(4):
                        for i in range(2):
                            load(sp, base, 72 + 2 * c + i, rows(w_ukv, 4, i, 2, c * 512), 512)
                    for c in range(4):
                        for i in range(8):
                            load(sp, base, 80 + 8 * c + i,
                                 rows(w_in, KT, i, 2, (COL_ZA if c < 2 else COL_ZB) + (c % 2) * 512), 512)
                    for c in range(4):
                        for i in range(8):
                            load(sp, base, 112 + 8 * c + i, rows(w_out, KT, i, 2, c * 512), 512)
                for n, tile_ in enumerate(MIX_TILES):
                    for i in range(4):
                        load(sp, U2, 4 * n + i, w_in2[:, 4 * i:4 * i + 4, tile_ * P:tile_ * P + 256], 256)
                for c in range(4):
                    for i in range(8):
                        k = 2 * OUT_PAIRS[i]
                        load(sp, U2, U_MIX + 8 * c + i, w_out2[:, k:k + 2, c * 512:(c + 1) * 512], 512)
                with sp.Fori(0, N_FFN) as turn_:
                    for half in range(2):
                        for i in range(4):
                            load(sp, turn_ * U_FFN + U3, 4 * half + i,
                                 w_up2[:, 4 * i:4 * i + 4, bass.ds(turn_ * 256 + half * D_FF, 256)], 256)
                for c in range(4):
                    for i in range(FT // 2):
                        load(sp, U4, (FT // 2) * c + i, w_down2[:, 2 * i:2 * i + 2, c * 512:(c + 1) * 512], 512)
                for ready, cols in ((final_row, slice(0, 3 * 512)), (final_last, slice(3 * 512, D))):
                    for t in range(T):
                        sp.wait_ge(ready[t], 1)
                        sp.dma_start(by_token(out)[:, t, cols], x[:, t, cols]).then_inc(stored, 16)
                sp.wait_ge(stored, 64)

            @block.gpsimd
            def _(pool):
                pool.dma_start(ffn_rows.rearrange("r (j p) -> r j p", p=P),
                               dram["ffn_rows"].rearrange("j r p -> r j p")).then_inc(rows_loaded, 16)
                pool.dma_start(fin_rows, dram["final_norm_g"].rearrange("(k p) -> k p", p=P)).then_inc(rows_loaded, 16)
                pool.dma_start(kvb[:, 1, 0:LAYERS * 4 * DQ],
                               dram["diff_lambda"].rearrange("l j d -> (l j d)").partition_broadcast(P))\
                    .then_inc(bias_loaded, 16)
                pool.dma_start(flip, dram["c_flip"]).then_inc(bias_loaded, 16)
                pool.dma_start(onehot, dram["c_onehot"]).then_inc(bias_loaded, 16)
                pool.dma_start(table, dram["rel_bias_table"]).then_inc(bias_loaded, 16)
                pool.dma_start(future, dram["c_future"]).then_inc(bias_loaded, 16)
                pool.dma_start(causal[:, :], dram["c_causal"]).then_inc(consts_loaded, 16)
                pool.dma_start(rope[:, :, :], dram["c_rope"].rearrange("(t p) n -> p t n", p=P))\
                    .then_inc(consts_loaded, 16)
                pool.wait_ge(bias_read, 1)
                pool.dma_start(bias_dram, bias_e).then_inc(bias_out, 16)
                pool.wait_ge(bias_out, 16)
                pool.dma_start(bias_up, bias_rows).then_inc(bias_back, 16)
                pool.wait_ge(acc_free[0], 1)
                pool.wait_ge(acc_free[1], 1)
                pool.dma_start(kv_dram, mem_kv1[:, :, :]).then_inc(kv_out, 16)

                pool.wait_ge(consts_loaded, 32)
                with pool.Fori(0, LAYERS) as layer:
                    pairs = layer * (C_LAYER // 2) + C_MEM // 2
                    step = Steps(pool, pool_step, layer * 19)
                    h2 = ROPE // 2
                    evacuated(pool, pairs, 8)
                    pool.wait_ge(tb_filled, layer * TB_LAYER + (TB_PRO + DIFF_TB[-1] + 1))
                    for t in range(T):
                        cos, sin = rope[:, t, 0:ROPE], rope[:, t, ROPE:2 * ROPE]
                        dst = kr2[:, t, :].rearrange("p (a e) -> p a e", a=2)
                        tmp = rope_tmp[:, t, 0:ROPE].rearrange("p (a e) -> p a e", a=2)
                        src = again(kr[:, t, :], 2)
                        step(pool.tensor_tensor(dst, src, again(cos, 2), ALU.mult))
                        step(pool.tensor_tensor(tmp, src[:, :, h2:ROPE], again(sin[:, 0:h2], 2), ALU.mult))
                        step(pool.tensor_tensor(dst[:, :, 0:h2], dst[:, :, 0:h2], tmp, ALU.add))
                        step(pool.tensor_tensor(tmp, src[:, :, 0:h2], again(sin[:, h2:ROPE], 2), ALU.mult))
                        step(pool.tensor_tensor(dst[:, :, h2:ROPE], dst[:, :, h2:ROPE], tmp, ALU.add))
                    evacuated(pool, pairs, 10)
                    evacuated(pool, pairs, 11)
                    for t in range(T):
                        cos, sin = rope[:, t, 0:ROPE], rope[:, t, ROPE:2 * ROPE]
                        src = qb[:, t, :].rearrange("p (h e) -> p h e", h=HEADS)[:, :, NOPE:NOPE + ROPE]
                        dst = qr[:, t, :].rearrange("p (h e) -> p h e", h=HEADS)
                        tmp = rope_tmp[:, t, :].rearrange("p (h e) -> p h e", h=HEADS)
                        step(pool.tensor_tensor(dst, src, again(cos, HEADS), ALU.mult))
                        step(pool.tensor_tensor(tmp, src[:, :, h2:ROPE], again(sin[:, 0:h2], HEADS), ALU.mult))
                        step(pool.tensor_tensor(dst[:, :, 0:h2], dst[:, :, 0:h2], tmp, ALU.add))
                        step(pool.tensor_tensor(tmp, src[:, :, 0:h2], again(sin[:, h2:ROPE], HEADS), ALU.mult))
                        last = pool.tensor_tensor(dst[:, :, h2:ROPE], dst[:, :, h2:ROPE], tmp, ALU.add)
                        if t == 0:
                            step(last)
                        else:
                            last.then_inc(roped, 1)
                    assert step.n == 19
                pool.wait_ge(row_max, (2 * LAYERS - 1) * HEADS)
                pool.dma_start(gain_mid, dram["final_norm_g"].partition_broadcast(P)).then_inc(gmid_loaded, 16)
                evacuated(pool, PAIRS2, -2)
                evacuated(pool, PAIRS2, -1)
                pool.dma_start(mkv[:, :, :], kv_dram).then_inc(mix_loaded, 16)
                pool.dma_start(pool_c[:, :], dram["c_pool"]).then_inc(mix_loaded, 16)
                for i, (_, p0, n) in enumerate(sum(POOL_PIECES, [])):
                    if n < P:
                        pool.memset(pool_w[P - p0 - n:P - p0, i, :], 0.0).then_inc(pool_zeroed, 1)
                w_rows = dram["pool_w_2"].rearrange("l g c d -> (l g c) d")
                for i, (tile_, p0, n) in enumerate(sum(POOL_PIECES, [])):
                    pool.dma_start(pool_w[p0:p0 + n, i, :], w_rows[tile_ * P + p0:tile_ * P + p0 + n, :])\
                        .then_inc(mix_loaded, 16)
                pool.wait_ge(act_ready, N_FFN)
                pool.dma_start(gfin[:, :], dram["g_final_2"].partition_broadcast(P)).then_inc(gfin_loaded, 16)

            @block.tensor
            def _(pe):
                pe.wait_ge(ident_loaded, 16)
                pe.wait_ge(par_loaded, 16)
                pe.transpose(acc[:, 2, 0:G_ROWS], par_rows, ident[0:G_ROWS, 0:G_ROWS]).then_inc(par_filled, 1)

                def turn_in(g):
                    if g < 8:
                        c, t = g // 2, g % 2
                        pe.wait_ge(mem_loaded[c], 16)
                        turn(pe, g, lambda i: mem[:, t, (4 * c + i) * P:(4 * c + i + 1) * P], g % 4, 3)
                    else:
                        c = (g - 8) // 2
                        pe.wait_ge(x_loaded[c], 16)
                        turn(pe, g, x_block(c, g % 2), g % 4, 3)

                for g in range(4):
                    turn_in(g)
                for j in range(U_MEM):
                    c, i = j // 8, j % 8
                    if c == 0 and i % 2 == 0:
                        pe.wait_ge(turn_lo, i + 2)
                    if j == 8:
                        pe.wait_ge(par_read, 2)
                        pe.wait_ge(bias_read, 1)
                    product_rows(pe, 0, j, mT, 2 * i, 2, 512, c, i == 0, i == 7)
                    if j < 4 or 6 <= j < 12:
                        turn_in(4 + j if j < 4 else 2 + j)
                    if j == 1:
                        pe.wait_ge(rows_loaded, 32)
                        pe.wait_ge(par_read, 1)
                        pe.transpose(acc[:, 2, G_FIN:G_ALL], fin_rows, ident[0:KT, 0:KT])
                        for i in range(TAPS + 1):
                            mm = pe.transpose(acc[:, 3, i * P:i * P + FFN_ROWS], ffn_rows[:, i * P:(i + 1) * P],
                                              ident[0:FFN_ROWS, 0:FFN_ROWS])
                        mm.then_inc(par_filled, 1)
                    if j == 4:
                        pe.wait_ge(bias_loaded, 80)
                        pe.wait_ge(par_read, 2)
                        pe.matmul(acc[0:HEADS, 2, 0:SEQ + P], table, onehot, start=True, stop=True)\
                          .then_inc(bias_filled, 1)
                    if j == 15:
                        pe.wait_ge(bias_back, 16)
                        pe.wait_ge(tb_free, TURNS_PRO)
                        for i in range(4):
                            mm = pe.matmul(aux[:, i, :], flip, kvb[:, 0, i * 512:(i + 1) * 512], start=True, stop=True)
                        mm.then_inc(tb_filled, 1)

                with pe.Fori(0, LAYERS) as layer:
                    base = layer * U_LAYER + U_MEM
                    pairs = layer * (C_LAYER // 2) + C_MEM // 2
                    tb0 = layer * TB_LAYER + TB_PRO
                    gain0 = layer * GAIN_LAYER + TURNS_PRO
                    pv0 = layer * (4 * HEADS)
                    head0 = layer * (2 * HEADS)

                    def turn_weights(n, cols):
                        if n > 0:
                            pe.wait_ge(pv_free, pv0 + n)
                        for i, col in enumerate(cols):
                            mm = pe.transpose(pv[:, i * P:(i + 1) * P], s[:, col:col + P], ident[:, :])
                        mm.then_inc(pv_filled, 1)

                    def outputs(n, val):
                        pe.wait_ge(pv_free, pv0 + n)
                        pe.matmul(pv[:, 0:P], pT[:, 0:P], val(0), start=True, stop=False)
                        pe.matmul(pv[:, 0:P], pT[:, P:2 * P], val(1), start=False, stop=True)
                        pe.matmul(pv[:, P:2 * P], pT[:, 2 * P:3 * P], val(0), start=True, stop=True)\
                            .then_inc(pv_filled, 1)

                    def diff_scores(h):
                        pe.wait_ge(tb_free, tb0 + (DIFF_TB[h] + 1))
                        if h > 0:
                            pe.wait_ge(row_max, head0 + h)
                        for col, q, keys in ((0, 1, SEQ), (SEQ, 0, P)):
                            for m, bank in ((0, sc1), (1, sc0)):
                                e = slice(m * DQ, (m + 1) * DQ)
                                mm = pe.matmul(bank[:, col:col + keys], qkT[e, q * P:(q + 1) * P],
                                               qkT[e, 2 * P:2 * P + keys], start=True, stop=True)
                        mm.then_inc(scores_ready, 1)

                    def diff_turn_weights(h):
                        pe.wait_ge(probs_ready, layer * HEADS + (h + 1))
                        turn_weights(2 * h, (0, P, 2 * SEQ))

                    def diff_outputs(h):
                        outputs(2 * h + 1, lambda k: kz[:, k, WIDTH + h * DV:WIDTH + (h + 1) * DV])

                    def mla_scores(h):
                        pe.wait_ge(tb_free, tb0 + (MLA_TB[h] + 1))
                        pe.wait_ge(row_max, head0 + (HEADS + h))
                        e = slice((h % 2) * ROPE, (h % 2 + 1) * ROPE)
                        for col, q, keys in ((0, 1, SEQ), (SEQ, 0, P)):
                            o = sc1[:, col:col + keys]
                            pe.matmul(o, qkT[:, q * P:(q + 1) * P], qkT[:, 2 * P:2 * P + keys], start=True, stop=False)
                            mm = pe.matmul(o, qrT[e, h // 2, q * P:(q + 1) * P], krT[e, 0:keys],
                                           start=False, stop=True)
                        mm.then_inc(scores_ready, 1)

                    def mla_turn_weights(h):
                        pe.wait_ge(rsum_ready, layer * HEADS + (h + 1))
                        turn_weights(2 * HEADS + 2 * h, (0, P, SEQ))

                    def mla_outputs(h):
                        v = h * (NOPE + DV) + NOPE
                        outputs(2 * HEADS + 2 * h + 1, lambda k: kvb[:, k, v:v + DV])

                    def diff_block(h):
                        return lambda i: (qa if i < 2 else kz)[:, i % 2, h * DV:(h + 1) * DV]

                    def mla_block(h):
                        def block_(i):
                            if i < 2:
                                return qb[:, i, h * (NOPE + ROPE):h * (NOPE + ROPE) + NOPE]
                            return kvb[:, i - 2, h * (NOPE + DV):h * (NOPE + DV) + NOPE]
                        return block_

                    def gated_block(g, t):
                        if g < 2:
                            return lambda i: qa[:, t, (4 * g + i) * DV:(4 * g + i + 1) * DV]
                        v = lambda i: (4 * (g - 2) + i) * (NOPE + DV)
                        return lambda i: kvb[:, t, v(i):v(i) + DV]

                    def z_heads(u):
                        h, r = (u - 2) // 4, (u - 2) % 4
                        if u >= 2 and r == 0:
                            if 0 < h <= HEADS:
                                mla_turn_weights(h - 1)
                            if h < HEADS:
                                turn(pe, tb0 + MLA_TB[h], mla_block(h))
                        if u >= 2 and r == 1:
                            if 0 < h <= HEADS:
                                mla_outputs(h - 1)
                            if h < HEADS:
                                mla_scores(h)
                        if u in GATE_TURN:
                            g, t, use = GATE_TURN[u]
                            pe.wait_ge(gated, layer * 8 + (2 * g + t + 1))
                            turn(pe, tb0 + use, gated_block(g, t))

                    for c in range(2):
                        banks_free(pe, pairs, c)
                        for i in range(8):
                            if c == 0 and i in (0, 6):
                                pe.wait_ge(turn_lo, gain0 + (2 if i else 0))
                            product_rows(pe, base, 8 * c + i, xT, 2 * i, 2, 512, c, i == 0, i == 7)
                            if c == 0 and i in (2, 3):
                                pe.wait_ge(x_loaded[3], 16)
                                evacuated(pe, pairs, -1)
                                turn(pe, tb0 + (i - 2), x_block(3, i - 2))
                    with pe.Fori(0, 2) as half:
                        for c in range(2):
                            banks_free(pe, pairs + half, 2 + c)
                            for i in range(8):
                                product_rows(pe, base + half * 16, 16 + 8 * c + i, xT, 2 * i, 2, 512, c, i == 0, i == 7)
                    for u in range(32):
                        if u < 18:
                            c, i, last_i = u // 8, u % 8, 7 if u < 16 else 1
                        else:
                            c, i, last_i = 3 + (u - 18) // 2, u % 2, 1
                        if i == 0:
                            banks_free(pe, pairs, 6 + c)
                        if u in (18, 24):
                            pe.wait_ge(turn_lo, gain0 + (4 if u == 18 else 6))
                        if u < 16:
                            product_rows(pe, base, 48 + u, xT, 2 * i, 2, 512, c % 2, i == 0, i == last_i)
                        elif u < 18:
                            product_rope_key(pe, base, 48 + u, 8 * i, i == 0, i == last_i)
                        else:
                            product_rows(pe, base, 48 + u, mT, (0 if u < 24 else 4) + 2 * i, 2, 512, c % 2,
                                         i == 0, i == last_i)
                        if u == 18:
                            pe.wait_ge(key_summed, layer + 1)
                            for t in range(T):
                                mm = pe.matmul(acc[:, 1, t * ROPE:(t + 1) * ROPE], krT[0:ROPE, t * P:(t + 1) * P],
                                               ident[0:ROPE, 0:ROPE], start=True, stop=True)
                            mm.then_inc(key_turned, 1)
                        h, r = u // 4, u % 4
                        if u == 0:
                            evacuated(pe, pairs, 4)
                            evacuated(pe, pairs, 5)
                        if r == 0:
                            if h > 0:
                                diff_turn_weights(h - 1)
                            turn(pe, tb0 + DIFF_TB[h], diff_block(h))
                        if r == 1:
                            if h > 0:
                                diff_outputs(h - 1)
                            diff_scores(h)
                        if u in C_TURN:
                            j, t, use = C_TURN[u]
                            evacuated(pe, pairs, 6 + j)
                            turn(pe, tb0 + use, lambda i: qb[:, t, j * RANK + i * P:j * RANK + (i + 1) * P])
                    for u in range(32):
                        c, i = u // 8, u % 8
                        if i == 0:
                            banks_free(pe, pairs, 16 + c)
                        product_rows(pe, base, 80 + u, xT, 2 * i, 2, 512, c % 2, i == 0, i == 7)
                        if u == 0:
                            diff_turn_weights(HEADS - 1)
                            pe.wait_ge(roped, layer + 1)
                            turn(pe, tb0 + QR_TB, lambda i: qr[:, i % 2, (i // 2) * P:(i // 2 + 1) * P])
                        if u == 1:
                            pe.wait_ge(pv_free, pv0 + (2 * HEADS - 1))
                            for t in range(T):
                                pe.transpose(pv[:, (2 + t) * P:(3 + t) * P], kr2[:, t, :], ident[:, :])
                            diff_outputs(HEADS - 1)
                            turn(pe, tb0 + (QR_TB + 1), lambda i: qr[:, i % 2, (2 + i // 2) * P:(3 + i // 2) * P])
                        z_heads(u)
                    for u in range(32):
                        c, i = u // 8, u % 8
                        if i == 0:
                            banks_free(pe, pairs, 20 + c)
                        if u in (0, 6):
                            pe.wait_ge(tb_free, tb0 + (29 if u == 0 else 31))
                        product_rows(pe, base, 112 + u, mT, 2 * i, 2, 512, c % 2, i == 0, i == 7,
                                     (lambda: pe.wait_ge(tb_free, tb0 + 32)) if u == 6 else None)
                        if u < 8:
                            z_heads(32 + u)
                        if c > 0 and i in (2, 3):
                            evacuated(pe, pairs, 20 + c - 1)
                            turn(pe, tb0 + (X_TB + 2 * (c - 1) + i - 2), x_block(c - 1, i - 2))

                def x_last_chunk(tb_first, pairs_now, t):
                    evacuated(pe, pairs_now, -1)
                    turn(pe, tb_first + t, x_block(3, t))

                def spread_rstd(rb, n):
                    pe.wait_ge(rb_ready, n)
                    for t in range(T):
                        mm = pe.matmul(sc0[:, t * P:(t + 1) * P], rb[:, t, :], ident[:, :], start=True, stop=True)
                    mm.then_inc(rb_filled, 1)

                def pool_matmul(g):
                    pe.wait_ge(pooled_ready, 3 if g else 2)
                    if g == 0:
                        pe.wait_ge(pool_zeroed, 4)
                        pe.wait_ge(tb_free, TB2 + 4)
                    if g == 1:
                        pe.wait_ge(xo_lo, XHEADS)
                    if g == 2:
                        pe.wait_ge(pool_scaled, 1)
                    bank = pv if g == 1 else tb
                    for group, pieces in enumerate(POOL_PIECES):
                        first_channel = 0
                        for tile_, p0, n in pieces:
                            if tile_ // 2 == g:
                                col = (tile_ % 2) * SEQ
                                for k, (kt, _, _) in enumerate(pieces):
                                    mm = pe.matmul(bank[p0:p0 + n, col:col + SEQ],
                                                   pool_w[:, 2 * group + k, first_channel:first_channel + n],
                                                   zT[:, 6 + kt, :],
                                                   start=k == 0, stop=k == len(pieces) - 1)
                            first_channel += n
                    mm.then_inc(pool_filled, 1)

                def cross_heads(u):
                    for h in range(XHEADS):
                        sc = sc1 if h % 2 == 0 else sc0
                        if u == X_SCORE[h]:
                            pe.wait_ge(queries_ready, 1 + h // 2)
                            if h == 0:
                                pe.wait_ge(tb_free, TB2 + 4)
                            if h >= 2:
                                pe.wait_ge(xexp_done, h - 1)
                            for t in range(T):
                                mm = pe.matmul(sc[:, t * SEQ:(t + 1) * SEQ], zT[:, 24 + h, t * P:(t + 1) * P],
                                               mkT[:, h, :], start=True, stop=True)
                            mm.then_inc(xs_ready, 1)
                        if u == X_TURN[h]:
                            pe.wait_ge(xprob_ready, h + 1)
                            if h > 0:
                                pe.wait_ge(xo_lo, h)
                            for k in range(T):
                                for t in range(T):
                                    mm = pe.transpose(pv[:, k * SEQ + t * P:k * SEQ + (t + 1) * P],
                                                      xe[:, h % 2, t, k * P:(k + 1) * P], ident[:, :])
                            mm.then_inc(xpt_filled, 1)
                        if u == X_OUT[h]:
                            pe.wait_ge(xpt_ready, h + 1)
                            v = D_XATT + h * P
                            for k in range(T):
                                mm = pe.matmul(pv[:, 0:SEQ], mkv[:, k, v:v + P], xpT[:, k, :],
                                               start=k == 0, stop=k == T - 1)
                            mm.then_inc(xo_filled, 1)

                for u in range(U_MIX):
                    n, i = u // 4, u % 4
                    if i == 0:
                        banks_free(pe, PAIRS2, n)
                    if u in (0, 3):
                        pe.wait_ge(turn_lo, GAIN2 + (2 if u else 0))
                    product_cols(pe, U2, u, 4 * i, n % 2, i == 0, i == 3)
                    if u in (0, 1):
                        x_last_chunk(TB2, PAIRS2, u)
                    if u == 10:
                        spread_rstd(rb2, 1)
                    if u in (10, 11):
                        pe.wait_ge(mix_loaded, 16 * (2 + N_PIECES))
                        g = u - 10
                        turn(pe, TB2 + 2 + g, lambda i: mkv[:, i % 2, (2 * g + i // 2) * P:(2 * g + i // 2 + 1) * P])
                    if u in POOL_OUT:
                        pool_matmul(POOL_OUT.index(u))
                    cross_heads(u)
                for u in range(U_OUT):
                    c, i = u // 8, u % 8
                    if i == 0:
                        banks_free(pe, PAIRS2, 14 + c)
                    if c == 0:
                        if i < 3:
                            pe.wait_ge(conv_lo, i + 1)
                        elif i < 5:
                            pe.wait_ge(xo_lo, 2 * (i - 2))
                        else:
                            pe.wait_ge(pool_lo, i - 4)
                    product_rows(pe, U2, U_MIX + u, mT, 2 * OUT_PAIRS[i], 2, 512, c % 2, i == 0, i == 7)
                    if U_MIX + u in POOL_OUT:
                        pool_matmul(POOL_OUT.index(U_MIX + u))
                    if c > 0 and i in (2, 3):
                        if c == 1 and i == 2:
                            pe.wait_ge(pool_scaled, CT // 2)
                        evacuated(pe, PAIRS2, 14 + c - 1)
                        turn(pe, TB2 + 4 + 2 * (c - 1) + i - 2, x_block(c - 1, i - 2))
                def ffn_turn(turn_):
                    first = isinstance(turn_, int)
                    for half in range(2):
                        banks_free(pe, turn_ + PAIRS3, half)
                        for i in range(4):
                            if first and half == 0 and i in (0, 3):
                                pe.wait_ge(turn_lo, GAIN3 + (2 if i else 0))
                            product_cols(pe, turn_ * U_FFN + U3, 4 * half + i, 4 * i, half, i == 0, i == 3)
                            if first and half == 0 and i in (0, 1):
                                x_last_chunk(TB3, PAIRS3, i)
                            if first and half == 1 and i == 0:
                                spread_rstd(rb3, 2)

                ffn_turn(0)
                with pe.Fori(1, N_FFN) as turn_:
                    ffn_turn(turn_)
                for c in range(4):
                    banks_free(pe, PAIRS4, c)
                    for i in range(FT // 2):
                        if c == 0:
                            pe.wait_ge(act_ready, i + 1)
                        product_rows(pe, U4, (FT // 2) * c + i, act_T, 2 * i, 2, 512, c % 2, i == 0, i == FT // 2 - 1)

            @block.scalar
            def _(act):
                def turned_in(g):
                    tile_, k = (mT, g) if g < 8 else (xT, g - 8)
                    turn_round(act, g, token_part(tile_, k // 2, k % 2, 0), g % 2)

                for g, units in ((0, ()), (1, (0,)), (2, ()), (3, (1, 2))):
                    turned_in(g)
                    for j in units:
                        round_unit(act, 0, j)
                m_step = Steps(act, m_squared)
                x_step = Steps(act, x_squared)
                for j in range(U_MEM):
                    if 1 <= j < 5:
                        turned_in(3 + j)
                    round_unit(act, 0, j + LEAD)
                    if 8 <= j < 14:
                        turned_in(j)
                    if 2 <= j < 6:
                        c = j - 2
                        for t in range(T):
                            m_step(act.activation(junk[:, :], mem[:, t, c * 512:(c + 1) * 512], ACT.Square,
                                                  accum_out=sumsq_m[:, t, c:c + 1]))
                    if j == 5:
                        act.wait_ge(dots_ready, 1)
                        act.activation(dots[:, :], dots[:, :], ACT.Exp).then_inc(exp_dots, 1)
                    if 10 <= j < 16:
                        square_x(x_step, act, (j - 10) // 2, ((j - 10) % 2,))
                act.wait_ge(tb_filled, TB_PRO)
                act.activation(bias[:, :, :].rearrange("p h k -> p (h k)"), aux[:, :, :].rearrange("p b k -> p (b k)"),
                               ACT.Copy).then_inc(tb_free, 1)

                with act.Fori(0, LAYERS) as layer:
                    quads = layer * (U_LAYER // RING) + U_MEM // RING
                    pairs = layer * (C_LAYER // 2) + C_MEM // 2
                    tb0 = layer * TB_LAYER + TB_PRO
                    pv0 = layer * (4 * HEADS)
                    head0 = layer * (2 * HEADS)
                    c_step = Steps(act, c_squared, layer * 4)
                    o_step = Steps(act, o_squared, layer * (2 * HEADS))
                    x_step = Steps(act, x_squared, layer * SQ_PRO + SQ_PRO)

                    def rounded(j):
                        round_unit(act, quads, j + LEAD, layer_unit_size(j + LEAD))

                    def copy_bank(use, dst):
                        act.wait_ge(tb_filled, tb0 + (use + 1))
                        act.activation(dst, tb, ACT.Copy).then_inc(tb_free, 1)

                    def exps(h, parts):
                        act.wait_ge(row_max, head0 + (h + 1))
                        for col, n, r in parts:
                            ins = act.activation(s[:, col:col + n], s[:, col:col + n], ACT.Exp,
                                                 bias=neg_max[:, r:r + 1], accum_out=row_sum[:, r:r + 1])
                        ins.then_inc(exps_done, 1)

                    def copy_weights(n):
                        act.wait_ge(pv_filled, pv0 + (n + 1))
                        act.activation(pT[:, :], pv[:, 0:3 * P], ACT.Copy).then_inc(pv_free, 1)

                    def diff_output(h):
                        act.wait_ge(pv_filled, pv0 + (2 * h + 2))
                        for t, col, r in ((1, 0, 0), (0, P, 2)):
                            o_step(act.activation(junk[:, 0:P], pv[:, col:col + P], ACT.Square,
                                                  scale=inv_sum[:, r:r + 1],
                                                  accum_out=sumsq_o[:, T * h + t:T * h + t + 1]))
                        for t, col, r in ((1, 0, 0), (0, P, 2)):
                            ins = act.activation(qa[:, t, h * DV:(h + 1) * DV], pv[:, col:col + P], ACT.Copy,
                                                 scale=inv_sum[:, r:r + 1])
                        if h == HEADS - 1:
                            ins = act.activation(krT[:, :], pv[:, 2 * P:4 * P], ACT.Copy)
                        ins.then_inc(pv_free, 1)

                    def mla_output(h):
                        act.wait_ge(pv_filled, pv0 + (2 * HEADS + 2 * h + 2))
                        v = h * (NOPE + DV)
                        for t, col, r in ((1, 0, 0), (0, P, 1)):
                            ins = act.activation(kvb[:, t, v:v + DV], pv[:, col:col + P], ACT.Copy,
                                                 scale=inv_sum[:, r:r + 1])
                        ins.then_inc(pv_free, 1)

                    def z_heads(u):
                        h, r = (u - 2) // 4, (u - 2) % 4
                        if u >= 2 and r == 0:
                            if 0 < h <= HEADS:
                                copy_weights(2 * HEADS + 2 * (h - 1))
                            if h < HEADS:
                                copy_bank(MLA_TB[h], qkT)
                        if u >= 2 and r == 1 and 0 < h <= HEADS:
                            mla_output(h - 1)
                        if u >= 2 and r == 2 and h < HEADS:
                            exps(HEADS + h, ((0, SEQ, 0), (SEQ, P, 1)))
                        if u > 0 and u % 8 == 0:
                            c = u // 8 - 1
                            evacuated(act, pairs, 16 + c)
                            z = kz[:, :, c * 512:(c + 1) * 512]
                            act.activation(z, z, ACT.Silu).then_inc(z_silu, 1)
                        if u in GATE_TURN:
                            g, t, use = GATE_TURN[u]
                            turn_round_plain(act, tb0 + use, token_part(mT, g, t, 0),
                                             subln_l[:, 0:1] if g < 2 else 1.0)

                    for j in range(16):
                        rounded(j)
                        if j == 1:
                            evacuated(act, pairs, -1)
                            square_x(Steps(act, x_squared, layer * SQ_PRO + 6), act, 3)
                        if j in (2, 3):
                            turn_round(act, tb0 + (j - 2), token_part(xT, 3, j - 2, 0))
                    with act.Fori(0, 2) as half:
                        for j in range(16):
                            round_unit(act, quads + half * 4, 16 + j + LEAD)
                    for u in range(32):
                        rounded(48 + u)
                        h, r = u // 4, u % 4
                        if r == 0:
                            if h > 0:
                                copy_weights(2 * (h - 1))
                            copy_bank(DIFF_TB[h], qkT)
                        if r == 1 and h > 0:
                            diff_output(h - 1)
                        if r == 2:
                            exps(h, ((0, SEQ, 0), (SEQ, SEQ, 1), (2 * SEQ, P, 2), (2 * SEQ + P, P, 3)))
                        if u in (8, 16):
                            j = u // 8 - 1
                            evacuated(act, pairs, 6 + j)
                            for t in range(T):
                                c_step(act.activation(junk[:, :], qb[:, t, j * RANK:(j + 1) * RANK], ACT.Square,
                                                      accum_out=sumsq_c[:, T * j + t:T * j + t + 1]))
                        if u in C_TURN:
                            j, t, use = C_TURN[u]
                            turn_round(act, tb0 + use, token_part(mT, j, t, 0))
                        if u == 20 or (u > 20 and u % 2 == 1):
                            c = (u - 19) // 2
                            act.wait_ge(c_rstd, layer + 1)
                            multiplied(act, quads * 4, 48 + 19 + 2 * c)
                            for t in range(T):
                                r = (0 if c < 3 else T) + t
                                dst = qb[:, t, c * 512:(c + 1) * 512] if c < 3 else \
                                    kvb[:, t, (c - 3) * 512:(c - 2) * 512]
                                ins = act.activation(dst, acc[:, 2 * ((9 + c) % 2) + t, :], ACT.Copy,
                                                     scale=rstd_c[:, r:r + 1])
                            ins.then_inc(acc_free[(9 + c) % 2], 1)
                    for u in range(32):
                        rounded(80 + u)
                        if u == 0:
                            copy_weights(2 * (HEADS - 1))
                            copy_bank(QR_TB, qrT[:, 0:2, :].rearrange("p a k -> p (a k)"))
                        if u == 1:
                            diff_output(HEADS - 1)
                            copy_bank(QR_TB + 1, qrT[:, 2:4, :].rearrange("p a k -> p (a k)"))
                        z_heads(u)
                    for u in range(32):
                        rounded(112 + u)
                        if u < 8:
                            z_heads(32 + u)
                        c, i = u // 8, u % 8
                        if c > 0 and i in (2, 3):
                            turn_round(act, tb0 + (X_TB + 2 * (c - 1) + i - 2), token_part(xT, c - 1, i - 2, 0))
                        if c > 0 and i == 1:
                            evacuated(act, pairs, 20 + c - 1)
                            square_x(x_step, act, c - 1)

                def copy_half(half, base, j, pair, pairs_now, c):
                    multiplied(act, base, j)
                    evacuated(act, pairs_now, c - 1)
                    act.activation(half[:, :, :], acc[:, 2 * pair:2 * pair + 2, SEQ:2 * SEQ], ACT.Copy)\
                       .then_inc(half_copied, 1)

                def cross_heads(u):
                    for h in range(XHEADS):
                        sc = sc1 if h % 2 == 0 else sc0
                        if u == X_SCORE[h] + 1:
                            act.wait_ge(xmax_ready, h + 1)
                            for t in range(T):
                                ins = act.activation(xe[:, h % 2, t, :], sc[:, t * SEQ:(t + 1) * SEQ], ACT.Exp,
                                                     bias=xmax[:, h, t:t + 1], scale=X_SCALE,
                                                     accum_out=xsum[:, h, t:t + 1])
                            ins.then_inc(xexp_done, 1)
                        if u == X_TURN[h] + 1:
                            act.wait_ge(xpt_filled, h + 1)
                            act.activation(xpT[:, :, :].rearrange("p k t -> p (k t)"), pv, ACT.Copy)\
                               .then_inc(xpt_ready, 1)
                        if u == X_OUT[h] + 1:
                            act.wait_ge(xo_filled, h + 1)
                            act.activation(mT[:, 12 + h, 0, :], pv[:, 0:SEQ], ACT.Copy).then_inc(xo_hi, 1)

                def pool_round(u):
                    if u - 1 in POOL_OUT:
                        g = POOL_OUT.index(u - 1)
                        act.wait_ge(pool_scaled, g + 1)
                        act.activation(mT[:, 6 + 2 * g:8 + 2 * g, 0, :], pool_f[:, :, :], ACT.Copy).then_inc(pool_hi, 1)

                quads2 = U2 // RING
                x_step = Steps(act, x_squared, SQ_PRO * LAYERS + 6)
                for u in range(U_MIX):
                    round_unit(act, quads2, u + LEAD)
                    if u == 0:
                        evacuated(act, PAIRS2, -1)
                        square_x(x_step, act, 3)
                    if 4 <= u < 8:
                        act.wait_ge(x_normed, u - 3)
                        square_x(x_step, act, u - 4)
                    n, i = u // 4, u % 4
                    if u in (0, 1):
                        turn_round(act, TB2 + u, token_part(xT, 3, u, 0))
                    if u in (10, 11):
                        g = u - 10
                        act.wait_ge(tb_filled, TB2 + 3 + g)
                        act.activation(mkT[:, 2 * g:2 * g + 2, :].rearrange("p h k -> p (h k)"), tb,
                                       ACT.Copy).then_inc(tb_free, 1)
                    if i == 0 and n > 0:
                        copy_half(half2, U2, u - 1, (n - 1) % 2, PAIRS2, n - 1)
                    if i == 1 and 6 < n < 10:
                        g = n - 7
                        act.wait_ge(conv_ready, g + 1)
                        act.activation(mT[:, 2 * g:2 * g + 2, 0, :], zT[:, 12 + 2 * g:14 + 2 * g, :], ACT.Copy)\
                           .then_inc(conv_hi, 1)
                    pool_round(u)
                    cross_heads(u)
                for u in range(U_OUT):
                    round_unit(act, quads2, U_MIX + u + LEAD)
                    if u == 0:
                        copy_half(half2, U2, U_MIX - 1, 13 % 2, PAIRS2, 13)
                    pool_round(U_MIX + u)
                    c, i = u // 8, u % 8
                    if c > 0 and i in (2, 3):
                        turn_round(act, TB2 + 4 + 2 * (c - 1) + i - 2, token_part(xT, c - 1, i - 2, 0))
                    if c > 0 and i == 1:
                        evacuated(act, PAIRS2, 14 + c - 1)
                        square_x(x_step, act, c - 1)
                def tap2(turn_, back, half):
                    y = value if half else gate
                    act.wait_ge(sum_ready, turn_ * 2 + (half + 1 - 2 * back))
                    for k in range(2):
                        ins = act.activation(y[:, k, :], sum3[:, k, :], ACT.Identity, scale=taps[:, 2, half, k:k + 1],
                                             bias=taps[:, 3, half, k:k + 1])
                    ins.then_inc(tap2_done, 1)

                def copy_value(turn_):
                    copy_half(half3, turn_ * U_FFN + U3, -1, 1, turn_ + (PAIRS3 - 1), 1)

                def ffn_turn(turn_):
                    first = isinstance(turn_, int)
                    for half in range(2):
                        for i in range(4):
                            round_unit(act, turn_ * (U_FFN // RING) + U3 // RING, 4 * half + i + LEAD)
                            if first and half == 0 and i in (0, 1):
                                turn_round(act, TB3 + i, token_part(xT, 3, i, 0))
                                if i == 1:
                                    square_x(x_step, act, 3)
                            if half == 0 and not first:
                                if i == 0:
                                    copy_value(turn_)
                                if i == 1:
                                    tap2(turn_, 1, 1)
                            if i == 0 and half == 1:
                                copy_half(half3, turn_ * U_FFN + U3, 3, 0, turn_ + PAIRS3, 0)
                            if i == 1 + first and half == 1:
                                tap2(turn_, 0, 0)
                            if i == 2 + first and half == 1:
                                act.wait_ge(gate_conv, turn_ + 1)
                                act.activation(gate[:, :, :], gate[:, :, :], ACT.Silu).then_inc(gate_silu, 1)

                ffn_turn(0)
                with act.Fori(1, N_FFN) as turn_:
                    ffn_turn(turn_)
                for c in range(4):
                    for i in range(FT // 2):
                        j = (FT // 2) * c + i
                        if j + LEAD < U_DOWN:
                            round_unit(act, U4 // RING, j + LEAD)
                        if j == 0:
                            copy_value(N_FFN)
                        if j == 1:
                            tap2(N_FFN, 1, 1)
                        if c > 0 and i == 1:
                            evacuated(act, PAIRS4, c - 1)
                            square_x(x_step, act, c - 1)
                for t in range(T):
                    act.wait_ge(last_added, t + 1)
                    x_step(act.activation(junk[:, :], x[:, t, 3 * 512:D], ACT.Square, accum_out=sumsq_x[:, t, 3:4]))
                act.wait_ge(final_rstd, 1)
                act.activation(x[:, 1, 0:3 * 512], x[:, 1, 0:3 * 512], ACT.Copy, scale=rstd[:, 1:2])\
                   .then_inc(final_row[1], 1)

            @block.vector
            def _(dve):
                step = Steps(dve, dve_step)
                dve.wait_ge(par_filled, 1)
                dve.tensor_copy(par[:, 0:G_ROWS], acc[:, 2, 0:G_ROWS]).then_inc(par_read, 1)
                dve.wait_ge(par_read, 1)

                def scale_in(g):
                    k = G_MEM + 4 * (g // 2) if g < 8 else G_NORM + 4 * ((g - 8) // 2)
                    turn_scale(dve, g, g - 1, par[:, k:k + 4], g % 2, g % 4)

                def rest_in(g):
                    tile_, k = (mT, g) if g < 8 else (xT, g - 8)
                    turn_rest(dve, g, token_part(tile_, k // 2, k % 2, 0), token_part(tile_, k // 2, k % 2, 1), g % 2)

                for pair in range(2):
                    for g in (2 * pair, 2 * pair + 1):
                        scale_in(g)
                    for g in (2 * pair, 2 * pair + 1):
                        rest_in(g)
                    rest_unit(dve, 0, pair)
                rest_unit(dve, 0, 2)
                for j in range(U_MEM):
                    if 1 <= j < 5:
                        scale_in(3 + j)
                        rest_in(3 + j)
                    rest_unit(dve, 0, j + LEAD)
                    if 7 <= j < 13:
                        scale_in(1 + j)
                    if 8 <= j < 14:
                        rest_in(j)
                    if j == 2:
                        dve.wait_ge(par_filled, 2)
                        dve.tensor_copy(par[:, G_FIN:G_ALL], acc[:, 2, G_FIN:G_ALL])
                        dve.tensor_copy(par_ffn[:, :, :],
                                        acc[:, 3, :].rearrange("p (j r) -> p j r", r=P)[:, :, 0:FFN_ROWS])\
                           .then_inc(par_read, 1)
                        dve.wait_ge(par_read, 2)
                        for l in range(LAYERS):
                            g = par[:, G_SUBLN + l:G_SUBLN + l + 1]
                            step(dve.tensor_scalar(g, g, 1.0 - lam_init(l), None, ALU.mult))
                        step(dve.tensor_tensor(par[:, G_MIX:G_MIX + KT], par[:, G_MIX:G_MIX + KT], par[:, G_FIN:G_ALL],
                                               ALU.mult))
                    if j == 4:
                        dve.wait_ge(bias_loaded, 80)
                        for l in range(LAYERS):
                            for i in range(2):
                                ins = dve.tensor_tensor_reduce(out=dot_tmp, in0=lam_raw[:, l, 2 * i, :],
                                                               in1=lam_raw[:, l, 2 * i + 1, :], scale=1.0, scalar=0.0,
                                                               op0=ALU.mult, op1=ALU.add,
                                                               accum_out=dots[:, 2 * l + i:2 * l + i + 1])
                                if (l, i) == (LAYERS - 1, 1):
                                    ins.then_inc(dots_ready, 1)
                                else:
                                    step(ins)
                    if j == 5:
                        dve.wait_ge(bias_filled, 1)
                        dve.tensor_tensor(bias_e, acc[0:HEADS, 2, 0:SEQ + P], future, ALU.add).then_inc(bias_read, 1)
                    if j == 6:
                        dve.wait_ge(m_squared, 8)
                        step(dve.tensor_reduce(sumsq_m2[:, :], sumsq_m[:, :, :], AX_X, ALU.add))
                        rsqrt(step, dve, rstd_m[:, :], sumsq_m2[:, :], T, D)
                    if j in (7, 15):
                        c = j // 8
                        evacuate_scaled(dve, 0, j, c, 512, lambda t: mem_kv1[:, t, c * 512:(c + 1) * 512], rstd_m)
                    if j == 8:
                        dve.wait_ge(exp_dots, 1)
                        for l in range(LAYERS):
                            step(dve.tensor_tensor(neg_lam[:, l:l + 1], dots[:, 2 * l + 1:2 * l + 2],
                                                   dots[:, 2 * l:2 * l + 1], ALU.subtract))
                            step(dve.tensor_scalar(neg_lam[:, l:l + 1], neg_lam[:, l:l + 1], -lam_init(l), None,
                                                   ALU.add))
                dve.wait_ge(kv_out, 16)
                dve.wait_ge(consts_loaded, 32)
                steps_before = step.n

                with dve.Fori(0, LAYERS) as layer:
                    base = layer * U_LAYER + U_MEM
                    pairs = layer * (C_LAYER // 2) + C_MEM // 2
                    tb0 = layer * TB_LAYER + TB_PRO
                    gain0 = layer * GAIN_LAYER + TURNS_PRO
                    turn0 = layer * TURN_LAYER + TURNS_PRO
                    head0 = layer * (2 * HEADS)
                    step = Steps(dve, dve_step, layer * DVE_STEPS_LAYER + steps_before)

                    def rest(j):
                        rest_unit(dve, base, j + LEAD, layer_unit_size(j + LEAD))

                    def diff_max(h):
                        dve.wait_ge(scores_ready, head0 + (h + 1))
                        two = lambda ap: ap.rearrange("p (m k) -> p m k", m=2)
                        dve.scalar_tensor_tensor(out=two(s[:, 0:2 * SEQ]), in0=aux[:, 1:3, 0:SEQ], scalar=DIFF_SCALE,
                                                 in1=again(bias[:, h, :], 2), op0=ALU.mult, op1=ALU.add)
                        step(dve.scalar_tensor_tensor(out=two(s[:, 2 * SEQ:3 * SEQ]), in0=aux[:, 1:3, SEQ:SEQ + P],
                                                      scalar=DIFF_SCALE, in1=again(bias[:, h, P:SEQ], 2),
                                                      op0=ALU.mult, op1=ALU.add))
                        dve.tensor_reduce(neg_max[:, 0:2], two(s[:, 0:2 * SEQ]), AX_X, ALU.max)
                        step(dve.tensor_reduce(neg_max[:, 2:4], two(s[:, 2 * SEQ:3 * SEQ]), AX_X, ALU.max))
                        dve.tensor_scalar(neg_max[:, :], neg_max[:, :], -1.0, None, ALU.mult).then_inc(row_max, 1)

                    def diff_weights(h):
                        dve.wait_ge(exps_done, head0 + (h + 1))
                        step(dve.reciprocal(inv_sum[:, :], row_sum[:, :]))
                        pairs_of = lambda ap, i: ap[:, :].rearrange("p (t m) -> p t m", m=2)[:, :, i]
                        step(dve.scalar_tensor_tensor(out=mix_f[:, :], in0=pairs_of(row_sum, 0), scalar=lam_l[:, 0:1],
                                                      in1=pairs_of(inv_sum, 1), op0=ALU.mult, op1=ALU.mult))
                        dve.scalar_tensor_tensor(out=s[:, 0:SEQ], in0=s[:, SEQ:2 * SEQ], scalar=mix_f[:, 0:1],
                                                 in1=s[:, 0:SEQ], op0=ALU.mult, op1=ALU.add)
                        dve.scalar_tensor_tensor(out=s[:, 2 * SEQ:2 * SEQ + P], in0=s[:, 2 * SEQ + P:3 * SEQ],
                                                 scalar=mix_f[:, 1:2], in1=s[:, 2 * SEQ:2 * SEQ + P],
                                                 op0=ALU.mult, op1=ALU.add).then_inc(probs_ready, 1)

                    def mla_max(h):
                        dve.wait_ge(scores_ready, head0 + (HEADS + h + 1))
                        dve.tensor_scalar(s[:, 0:P], sc1[:, 0:P], MLA_SCALE, None, ALU.mult)
                        two = lambda ap: ap.rearrange("p (m k) -> p m k", m=2)
                        step(dve.scalar_tensor_tensor(out=two(s[:, P:3 * P]), in0=two(sc1[:, P:3 * P]), scalar=MLA_SCALE,
                                                      in1=again(causal[:, :], 2), op0=ALU.mult, op1=ALU.add))
                        dve.tensor_reduce(neg_max[:, 0:1], s[:, 0:SEQ], AX_X, ALU.max)
                        step(dve.tensor_reduce(neg_max[:, 1:2], s[:, SEQ:SEQ + P], AX_X, ALU.max))
                        dve.tensor_scalar(neg_max[:, 0:2], neg_max[:, 0:2], -1.0, None, ALU.mult).then_inc(row_max, 1)

                    def mla_sums(h):
                        dve.wait_ge(exps_done, head0 + (HEADS + h + 1))
                        dve.reciprocal(inv_sum[:, 0:2], row_sum[:, 0:2]).then_inc(rsum_ready, 1)

                    def gate_outputs(g, t):
                        dve.wait_ge(z_silu, layer * 4 + (g + 1))
                        z = kz[:, t, g * 512:(g + 1) * 512].rearrange("p (h d) -> p h d", h=4)
                        if g < 2:
                            o = qa[:, t, g * 512:(g + 1) * 512].rearrange("p (h d) -> p h d", h=4)
                            r = rstd_o[:, :].rearrange("p (h t) -> p h t", t=T)[:, 4 * g:4 * g + 4, t]
                            step(dve.tensor_tensor(o, o, wide(r, DV), ALU.mult))
                        else:
                            dve.wait_ge(pv_free, layer * (4 * HEADS) + (2 * HEADS + 8 * (g - 1)))
                            o = kvb[:, t, :].rearrange("p (h e) -> p h e", h=HEADS)[:, 4 * (g - 2):4 * (g - 1), 0:DV]
                        dve.tensor_tensor(o, o, z, ALU.mult).then_inc(gated, 1)

                    def z_heads(u):
                        if u >= 3 and (u - 3) % 4 == 0 and (u - 3) // 4 < HEADS:
                            mla_max((u - 3) // 4)
                        if u >= 5 and (u - 5) % 4 == 0 and (u - 5) // 4 < HEADS:
                            mla_sums((u - 5) // 4)
                        if u % 8 == 7 and u < 32:
                            c = u // 8
                            evacuate_scaled(dve, base, 80 + u, c % 2, 512,
                                            lambda t: kz[:, t, c * 512:(c + 1) * 512], rstd)
                        for g, steps_ in enumerate(((9, 10), (17, 18), (25, 26), (35, 35))):
                            for t in range(T):
                                if u == steps_[t]:
                                    gate_outputs(g, t)
                        if u in GATE_TURN:
                            g, t, use = GATE_TURN[u]
                            turn_rest_plain(dve, turn0 + (6 + 2 * g + t), token_part(mT, g, t, 0), token_part(mT, g, t, 1),
                                            subln_l[:, 0:1] if g < 2 else 1.0)

                    for j in range(16):
                        rest(j)
                        if j == 1:
                            step(dve.tensor_scalar(lam_l[:, 0:1], neg_lam[:, bass.ds(layer, 1)], 1.0, None, ALU.mult))
                            step(dve.tensor_scalar(subln_l[:, :], par[:, bass.ds(layer + G_SUBLN, 1)], 1.0, None, ALU.mult))
                            step(dve.tensor_scalar(gain_c[:, 0:4], par[:, bass.ds(layer * 4 + G_Q, 4)], 1.0, None, ALU.mult))
                            step(dve.tensor_scalar(gain_c[:, 4:8], par[:, bass.ds(layer * 4 + G_KV, 4)], 1.0, None, ALU.mult))
                        if j in (2, 3):
                            turn_scale(dve, tb0 + (j - 2), gain0 + (j - 2), par[:, bass.ds(layer * KT + 12, 4)])
                            turn_rest(dve, turn0 + (j - 2), token_part(xT, 3, j - 2, 0), token_part(xT, 3, j - 2, 1))
                        if j == 4:
                            x_rstd(step, dve, layer * SQ_PRO + SQ_PRO)
                        if j in (7, 15):
                            c = j // 8
                            evacuate_scaled(dve, base, j, c, 512, lambda t: qa[:, t, c * 512:(c + 1) * 512], rstd)
                    with dve.Fori(0, 2) as half:
                        for j in range(16):
                            rest_unit(dve, base + half * 16, 16 + j + LEAD)
                            if j in (7, 15):
                                c = j // 8
                                evacuate_scaled(dve, base + half * 16, 16 + j, c, 512,
                                                lambda t: kz[:, t, bass.ds(half * WIDTH + c * 512, 512)], rstd)
                    dve.wait_ge(tb_free, TB_PRO)
                    for u in range(32):
                        if u == 18:
                            multiplied(dve, base, 48 + 17)
                            step(dve.tensor_copy(krT[0:ROPE, :], acc[0:ROPE, 0, SEQ:2 * SEQ]))
                            dve.tensor_tensor(krT[0:ROPE, :], acc[0:ROPE, 0, 0:SEQ], krT[0:ROPE, :], ALU.add)\
                               .then_inc(key_summed, 1)
                        if u == 19:
                            dve.wait_ge(key_turned, layer + 1)
                            dve.tensor_tensor(kr[:, :, :], acc[:, 1, 0:T * ROPE].rearrange("p (t e) -> p t e", t=T),
                                              wide(rstd[:, :], ROPE), ALU.mult).then_inc(acc_free[0], 1)
                        if u % 4 == 3:
                            diff_weights(u // 4)
                        rest(48 + u)
                        if u in (7, 15):
                            j = u // 8
                            evacuate_scaled(dve, base, 48 + u, j, 512, lambda t: qb[:, t, j * RANK:(j + 1) * RANK], rstd)
                        if u in C_TURN:
                            j, t, use = C_TURN[u]
                            turn_scale(dve, tb0 + use, gain0 + (2 + 2 * j + t), gain_c[:, 4 * j:4 * j + 4])
                            turn_rest(dve, turn0 + (2 + 2 * j + t), token_part(mT, j, t, 0), token_part(mT, j, t, 1))
                        if u % 4 == 1:
                            diff_max(u // 4)
                        if u == 19:
                            dve.wait_ge(c_squared, layer * 4 + 4)
                            rsqrt(step, dve, rstd_c[:, :], sumsq_c[:, :], 4, RANK, done=c_rstd)
                    for u in range(32):
                        rest(80 + u)
                        if u == 2:
                            dve.wait_ge(o_squared, layer * (2 * HEADS) + 2 * HEADS)
                            rsqrt(step, dve, rstd_o[:, :], sumsq_o[:, :], HEADS * T, DV)
                        z_heads(u)
                    for u in range(32):
                        rest(112 + u)
                        if u < 8:
                            z_heads(32 + u)
                        c, i = u // 8, u % 8
                        if c > 0 and i in (2, 3):
                            k = 2 * (c - 1) + i - 2
                            turn_scale(dve, tb0 + (X_TB + k), gain0 + (6 + k),
                                       par[:, bass.ds(layer * KT + (KT + 4 * (c - 1)), 4)])
                            turn_rest(dve, turn0 + (14 + k), token_part(xT, c - 1, i - 2, 0),
                                      token_part(xT, c - 1, i - 2, 1))
                        if i == 7:
                            add_to_x(dve, base, 112 + u, c % 2, c)
                    assert step.n == DVE_STEPS_LAYER, step.n
                step = Steps(dve, dve_step, steps_before + LAYERS * DVE_STEPS_LAYER)

                def spread(rb, squares, also=None):
                    x_rstd(step, dve, squares)
                    if also is not None:
                        step(dve.tensor_tensor(rstd[:, :], rstd[:, :], also[:, :], ALU.mult))
                    for t in range(T):
                        ins = dve.tensor_scalar(rb[:, t, :], ident[:, :], 0.0, rstd[:, t:t + 1], ALU.mult, ALU.add)
                    ins.then_inc(rb_ready, 1)

                def spread_read(rbc, n):
                    dve.wait_ge(rb_filled, n)
                    step(dve.tensor_copy(rbc[:, :], sc0[:, 0:SEQ]))

                def both_halves(half, total, pair, copied):
                    dve.wait_ge(half_copied, copied)
                    dve.tensor_tensor(total, acc[:, 2 * pair:2 * pair + 2, 0:SEQ], half[:, :, :], ALU.add)\
                       .then_inc(acc_free[pair], 1)

                def conv_taps(y, u, tap, done=None):
                    if len(tap) > TAPS:
                        step(dve.tensor_scalar(y, u, tap[2], tap[3], ALU.mult, ALU.add))
                    else:
                        step(dve.tensor_scalar(y, u, tap[2], None, ALU.mult))
                    for d in (1, 2):
                        last = dve.scalar_tensor_tensor(out=y[:, d:SEQ], in0=u[:, 0:SEQ - d], scalar=tap[2 - d],
                                                        in1=y[:, d:SEQ], op0=ALU.mult, op1=ALU.add)
                        if d == 2 and done is not None:
                            last.then_inc(done, 1)
                        else:
                            step(last)

                def pool_sums(g):
                    v, s2, s4, s8, s16 = zT[:, 18:24, :], zT[:, 0:6, :], zT[:, 6:12, :], zT[:, 12:18, :], zT[:, 0:6, :]

                    def double(dst, src, first, d):
                        first = max(first, 2 * g)
                        if first < 2 * g + 2:
                            e = slice(first, 2 * g + 2)
                            dve.tensor_tensor(dst[:, e, d:SEQ], src[:, e, d:SEQ], src[:, e, 0:SEQ - d], ALU.add)
                            step(dve.tensor_copy(dst[:, e, 0:d], src[:, e, 0:d]))

                    double(s2, v, 0, 1)
                    double(s4, s2, 1, 2)
                    double(s8, s4, 3, 4)
                    double(s16, s8, 4, 8)
                    for tile_, p0, n, src in ((0, 0, P, s2), (1, 0, 64, s2), (1, 64, 64, s4), (2, 0, P, s4),
                                              (3, 0, P, s8), (4, 0, 64, s8), (4, 64, 64, s16), (5, 0, P, s16)):
                        e = slice(p0, p0 + n)
                        if tile_ // 2 == g:
                            step(dve.tensor_scalar(s4[e, tile_, :], src[e, tile_, :], pool_c[e, tile_:tile_ + 1], None,
                                                   ALU.mult))
                    chunk = slice(2 * g, 2 * g + 2)
                    early = s4[:, chunk, 0:16]
                    step(dve.tensor_tensor(early, early, pool_c[:, CT:CT + CT * 16].rearrange("p (t k) -> p t k", k=16)
                                           [:, chunk, :], ALU.mult))
                    dve.tensor_tensor(s4[:, chunk, :], s4[:, chunk, :], v[:, chunk, :], ALU.subtract)\
                       .then_inc(pooled_ready, 1)

                def pool_steps(u):
                    if u in POOL_SUMS:
                        g = POOL_SUMS.index(u)
                        if g == 0:
                            dve.wait_ge(mix_loaded, 16 * (2 + N_PIECES))
                        pool_sums(g)
                    if u - 1 in POOL_OUT:
                        g = POOL_OUT.index(u - 1)
                        dve.wait_ge(pool_filled, g + 1)
                        if g > 0:
                            dve.wait_ge(pool_lo, g)
                        bank = (pv if g == 1 else tb).rearrange("p (c t) -> p c t", c=2)
                        dve.tensor_tensor(pool_f[:, :, :], bank, wide(par[:, G_POOL + 2 * g:G_POOL + 2 * g + 2], SEQ),
                                          ALU.mult).then_inc(pool_scaled, 1)
                        dve.wait_ge(pool_hi, g + 1)
                        dve.tensor_tensor(mT[:, 6 + 2 * g:8 + 2 * g, 1, :], pool_f[:, :, :],
                                          mT[:, 6 + 2 * g:8 + 2 * g, 0, :].bitcast(F32), ALU.subtract).then_inc(pool_lo, 1)

                def mix_chunk(n):
                    tile_ = MIX_TILES[n]
                    pair = zT[:, tile_:tile_ + 2, :]
                    both_halves(half2, pair if n < 3 else sum2[:, :, :], n % 2, n + 1)
                    evacuated(dve, PAIRS2, n)
                    if N_QUERY <= n < N_POOL:
                        dve.tensor_tensor(pair, sum2[:, :, :], again(rbc2[:, :], 2), ALU.mult)\
                           .then_inc(queries_ready, 1)
                        dve.wait_ge(queries_ready, n - N_QUERY + 1)
                    elif n >= 3:
                        step(dve.tensor_tensor(pair, sum2[:, :, :], again(rbc2[:, :], 2), ALU.mult))
                    if 3 <= n < 6:
                        c_pair = zT[:, tile_ - 6:tile_ - 4, :]
                        step(dve.tensor_tensor(c_pair, c_pair, again(rbc2[:, :], 2), ALU.mult))
                        step(dve.tensor_tensor(c_pair, c_pair, pair, ALU.mult))
                    if 6 <= n < 9:
                        for k in range(2):
                            t_ = tile_ + k
                            taps_ = [par[:, G_CONV + j * CT + t_:G_CONV + j * CT + t_ + 1] for j in range(TAPS)]
                            conv_taps(zT[:, 12 + t_, :], zT[:, 6 + t_, :], taps_)
                        y = zT[:, 12 + tile_:14 + tile_, :]
                        dve.tensor_tensor(y, y, pair, ALU.mult).then_inc(conv_ready, 1)

                def cross_heads(u):
                    for h in range(XHEADS):
                        sc = sc1 if h % 2 == 0 else sc0
                        if u == X_SCORE[h] + 1:
                            dve.wait_ge(xs_ready, h + 1)
                            step(dve.tensor_reduce(xmax[:, h, :], sc.rearrange("p (t k) -> p t k", t=T), AX_X, ALU.max))
                            dve.tensor_scalar(xmax[:, h, :], xmax[:, h, :], -X_SCALE, None, ALU.mult)\
                               .then_inc(xmax_ready, 1)
                        if u == X_SCORE[h] + 2:
                            dve.wait_ge(xexp_done, h + 1)
                            step(dve.reciprocal(xinv[:, h, :], xsum[:, h, :]))
                            for t in range(T):
                                e = xe[:, h % 2, t, :]
                                ins = dve.tensor_scalar(e, e, xinv[:, h, t:t + 1], None, ALU.mult)
                            ins.then_inc(xprob_ready, 1)
                        if u == X_OUT[h] + 1:
                            dve.wait_ge(xo_hi, h + 1)
                            dve.tensor_tensor(mT[:, 12 + h, 1, :], pv[:, 0:SEQ], mT[:, 12 + h, 0, :].bitcast(F32),
                                              ALU.subtract).then_inc(xo_lo, 1)

                for u in range(U_MIX):
                    rest_unit(dve, U2, u + LEAD)
                    n, i = u // 4, u % 4
                    if u in (0, 1):
                        turn_scale(dve, TB2 + u, GAIN2 + u, par[:, G_MIX + 12:G_MIX + 16])
                        turn_rest(dve, TURN2 + u, token_part(xT, 3, u, 0), token_part(xT, 3, u, 1))
                    if u == 2:
                        x_rstd(step, dve, SQ_PRO * (1 + LAYERS))
                        step(dve.tensor_copy(rstd_mid[:, :], rstd[:, :]))
                    if 3 <= u < 7:
                        if u == 3:
                            dve.wait_ge(gmid_loaded, 16)
                            dve.wait_ge(tb_filled, TB2 + 2)
                        cols = slice((u - 3) * 512, (u - 2) * 512)
                        for t in range(T):
                            ins = dve.scalar_tensor_tensor(out=x[:, t, cols], in0=x[:, t, cols],
                                                           scalar=rstd_mid[:, t:t + 1], in1=gain_mid[:, cols],
                                                           op0=ALU.mult, op1=ALU.mult)
                        ins.then_inc(x_normed, 1)
                    if u == 8:
                        spread(rb2, SQ_PRO * (2 + LAYERS), rstd_mid)
                    if u == 11:
                        spread_read(rbc2, 1)
                    cross_heads(u)
                    if i == 0 and n > 0:
                        mix_chunk(n - 1)
                    if i == 2 and 6 < n < 10:
                        g = n - 7
                        dve.wait_ge(conv_hi, g + 1)
                        dve.tensor_tensor(mT[:, 2 * g:2 * g + 2, 1, :], zT[:, 12 + 2 * g:14 + 2 * g, :],
                                          mT[:, 2 * g:2 * g + 2, 0, :].bitcast(F32), ALU.subtract).then_inc(conv_lo, 1)
                    pool_steps(u)
                for u in range(U_OUT):
                    rest_unit(dve, U2, U_MIX + u + LEAD)
                    if u == 0:
                        mix_chunk(13)
                    pool_steps(U_MIX + u)
                    c, i = u // 8, u % 8
                    if c > 0 and i in (2, 3):
                        k = 2 * (c - 1) + i - 2
                        g = G_FFN + 4 * (c - 1)
                        turn_scale(dve, TB2 + 4 + k, GAIN2 + 2 + k, par[:, g:g + 4])
                        turn_rest(dve, TURN2 + 2 + k, token_part(xT, c - 1, i - 2, 0), token_part(xT, c - 1, i - 2, 1))
                    if i == 7:
                        add_to_x(dve, U2, U_MIX + u, c % 2, c)
                steps_before_ffn = step.base + step.n
                step.base, step.n = steps_before_ffn, 0

                def ffn_sums(turn_, back, half):
                    tiles = half * FT - 2 * back
                    cols = bass.ds(turn_ * 2 + tiles, 2)
                    step(dve.tensor_scalar(taps[:, :, half, :], par_ffn[:, :, cols], 1.0, None, ALU.mult))
                    both_halves(half3, sum3, half, turn_ * 2 + (14 + half + 1 - 2 * back))
                    evacuated(dve, turn_ + (PAIRS3 - back), half)
                    dve.tensor_tensor(sum3, sum3, again(rbc3[:, :], 2), ALU.mult).then_inc(sum_ready, 1)

                def ffn_conv(turn_, back, half, done=None):
                    y = value if half else gate
                    dve.wait_ge(tap2_done, turn_ * 2 + (half + 1 - 2 * back))
                    for d in (1, 2):
                        for k in range(2):
                            last = dve.scalar_tensor_tensor(out=y[:, k, d:SEQ], in0=sum3[:, k, 0:SEQ - d],
                                                            scalar=taps[:, 2 - d, half, k:k + 1], in1=y[:, k, d:SEQ],
                                                            op0=ALU.mult, op1=ALU.add)
                            if k == 1 and d == 1:
                                step(last)
                            elif k == 1:
                                if done is None:
                                    step(last)
                                else:
                                    last.then_inc(done, 1)

                def ffn_act(turn_, back):
                    dve.wait_ge(gate_silu, turn_ + (1 - back))
                    step(dve.tensor_tensor(value, value, gate, ALU.mult))
                    tiles = bass.ds(turn_ * 2 - 2 * back, 2)
                    hi = act_T[:, tiles, 0, :]
                    step(dve.tensor_scalar(hi, value, 1.0, None, ALU.mult))
                    dve.tensor_tensor(act_T[:, tiles, 1, :], value, hi.bitcast(F32), ALU.subtract).then_inc(act_ready, 1)

                def ffn_turn(turn_, first):
                    for half in range(2):
                        for i in range(4):
                            rest_unit(dve, turn_ * U_FFN + U3, 4 * half + i + LEAD)
                            if first and half == 0:
                                if i in (0, 1):
                                    turn_scale(dve, TB3 + i, GAIN3 + i, par[:, G_FFN + 12:G_FFN + 16])
                                    turn_rest(dve, TURN3 + i, token_part(xT, 3, i, 0), token_part(xT, 3, i, 1))
                                if i == 3:
                                    spread(rb3, SQ_PRO * (3 + LAYERS))
                            if half == 0 and not first:
                                if i == 0:
                                    ffn_sums(turn_, 1, 1)
                                if i == 1:
                                    ffn_conv(turn_, 1, 1)
                                if i == 2:
                                    ffn_act(turn_, 1)
                            if half == 1:
                                if i == first:
                                    if first:
                                        spread_read(rbc3, 2)
                                    ffn_sums(turn_, 0, 0)
                                if i == 1 + first:
                                    ffn_conv(turn_, 0, 0, gate_conv)
                                    dve.wait_ge(gate_conv, turn_ + 1)

                ffn_turn(0, True)
                assert step.n == FIRST_FFN_STEPS, step.n
                with dve.Fori(1, N_FFN) as turn_:
                    steps0 = steps_before_ffn + FIRST_FFN_STEPS - FFN_STEPS
                    step.base, step.n = turn_ * FFN_STEPS + steps0, 0
                    ffn_turn(turn_, False)
                    assert step.n == FFN_STEPS, step.n
                step.base, step.n = steps0 + N_FFN * FFN_STEPS, 0
                def apply_gain(c):
                    cols = slice(c * 512, (c + 1) * 512)
                    dve.wait_ge(x_squared, SQ_PRO * (3 + LAYERS) + 2 * (c + 1))
                    for t in range(T):
                        ins = dve.tensor_tensor(x[:, t, cols], x[:, t, cols], gfin[:, cols], ALU.mult)
                    ins.then_inc(gain_applied, 1)
                for c in range(4):
                    for i in range(FT // 2):
                        j = (FT // 2) * c + i
                        if j + LEAD < U_DOWN:
                            rest_unit(dve, U4, j + LEAD)
                        if j == 0:
                            ffn_sums(N_FFN, 1, 1)
                        if j == 1:
                            ffn_conv(N_FFN, 1, 1)
                        if j == 2:
                            ffn_act(N_FFN, 1)
                        if c > 0 and i == 4:
                            if c == 1:
                                dve.wait_ge(gfin_loaded, 16)
                            apply_gain(c - 1)
                    if c < 3:
                        add_to_x(dve, U4, (FT // 2) * (c + 1) - 1, c % 2, c)
                multiplied(dve, U4, U_DOWN - 1)
                last = slice(3 * 512, D)
                for t in range(T):
                    dve.tensor_tensor(x[:, t, last], acc[:, 2 + t, :], x[:, t, last], ALU.add).then_inc(last_added, 1)
                dve.wait_ge(gain_applied, 3)
                x_rstd(step, dve, SQ_PRO * (4 + LAYERS), final_rstd)
                dve.wait_ge(final_rstd, 1)
                dve.tensor_scalar(x[:, 0, 0:3 * 512], x[:, 0, 0:3 * 512], rstd[:, 0:1], None, ALU.mult)\
                   .then_inc(final_row[0], 1)
                for t in range(T):
                    dve.scalar_tensor_tensor(out=x[:, t, last], in0=x[:, t, last], scalar=rstd[:, t:t + 1],
                                             in1=gfin[:, last], op0=ALU.mult, op1=ALU.mult).then_inc(final_last[t], 1)


def kernel(**arrays):
    import concourse.bacc as _bacc
    from concourse.bass_utils import run_bass_kernel_spmd

    rows = lambda name: np.asarray(arrays[name]).reshape(-1, P)
    data = {n: np.asarray(arrays[n]) for n in (
        "x", "w_in", "diff_lambda", "rel_bias_table", "w_uq", "w_ukv", "w_out", "final_norm_g",
        "mem_2", "w_in_2", "pool_w_2", "w_kv_2", "w_out_2", "w_up_2", "w_down_2", "g_final_2")}
    data["par_rows"] = np.concatenate([rows(n) for n in (
        "norm_g", "g_mix_2", "g_ffn_2", "mla_q_norm_g", "mla_kv_norm_g", "pool_scale_2", "conv_w_2", "g_mem_2", "diff_subln_g")])
    data["ffn_rows"] = np.concatenate([rows("ffn_conv_w_2"), rows("ffn_conv_b_2")]).reshape(TAPS + 1, FFN_ROWS, P)
    data.update(shape_constants())

    nc = _bacc.Bacc("TRN2", target_bir_lowering=False, num_devices=1)
    dram = {n: nc.dram_tensor(n, list(a.shape), F32, kind="ExternalInput").ap() for n, a in data.items()}
    out = nc.dram_tensor("out", [1, SEQ, D], F32, kind="ExternalOutput")
    build(nc, dram, out.ap())
    nc.compile()
    r = run_bass_kernel_spmd(nc, [data], core_ids=[0])
    return r.results[0]["out"]
```
